# Optimizing a Trainium2 kernel written in Bass

```python
import math
import jax, jax.numpy as jnp
from jax import lax
import numpy as np

D_MODEL = 1024
BATCH = 1
SEQ = 2048
DEPTH = 2
DEC_BATCH = 8
DEC_SEQ = 4
PAST_LEN = 1024
PAGE_SIZE = 128

N_A_LAYERS = DEPTH // 2
N_B_LAYERS = DEPTH - N_A_LAYERS
D_A = 2 * D_MODEL
POOL_WINDOWS = (2, 4, 8, 16)
N_POOL_GROUPS = len(POOL_WINDOWS)
G_A = D_A // N_POOL_GROUPS
POOL_BUF = max(POOL_WINDOWS) - 1
N_HEADS = 8
HEAD_DIM = D_MODEL // N_HEADS // 2
KD = 2 * HEAD_DIM
VD = 2 * HEAD_DIM
D_B = N_HEADS * VD
Q_BLOCK = 128
SCALE = HEAD_DIM ** -0.5
EPS = 1e-6

kernel_name = 'yoco_pool_diffattn_decode_step'

def rmsnorm(x, g):
    xf = x.astype(jnp.float32)
    y = xf * lax.rsqrt(jnp.mean(xf * xf, axis=-1, keepdims=True) + EPS)
    return (y * g.astype(jnp.float32)).astype(x.dtype)

def alibi_slopes():
    return jnp.asarray(2.0 ** (-8.0 * np.arange(1, N_HEADS + 1) / N_HEADS), dtype=jnp.float32)

def multiscale_pool(u_ext, pos0):
    b, l, _ = u_ext.shape
    t = l - POOL_BUF
    c = jnp.concatenate([jnp.zeros((b, 1, D_A), jnp.float32), jnp.cumsum(u_ext, axis=1)], axis=1)
    pos = pos0 + jnp.arange(t, dtype=jnp.float32)
    outs = []
    for g, w in enumerate(POOL_WINDOWS):
        sl = slice(g * G_A, (g + 1) * G_A)
        hi = c[:, POOL_BUF + 1:POOL_BUF + 1 + t, sl]
        lo = c[:, POOL_BUF + 1 - w:POOL_BUF + 1 - w + t, sl]
        cnt = jnp.minimum(jnp.float32(w), pos + 1.0)
        outs.append((hi - lo) / cnt[None, :, None])
    pooled = jnp.concatenate(outs, axis=-1)
    return pooled - u_ext[:, POOL_BUF:]

def pool_layer(x, buf, pos0, g_norm, w_in, w_map, scale, w_out):
    b, t, _ = x.shape
    uz = rmsnorm(x, g_norm) @ w_in
    u, z = uz[..., :D_A], uz[..., D_A:]
    u_ext = jnp.concatenate([buf.astype(u.dtype), u], axis=1)
    mix = multiscale_pool(u_ext.astype(jnp.float32), pos0)
    mix = jnp.einsum('btgi,gio->btgo', mix.reshape(b, t, N_POOL_GROUPS, G_A), w_map.astype(jnp.float32))
    mix = (mix.reshape(b, t, D_A) * scale.astype(jnp.float32)).astype(x.dtype)
    y = (mix * jax.nn.silu(z)) @ w_out
    return x + y, u_ext[:, -POOL_BUF:]

def shared_kv(x, g_norm, w_kv):
    b, t, _ = x.shape
    kv = rmsnorm(x, g_norm) @ w_kv
    k = kv[..., :N_HEADS * KD].reshape(b, t, N_HEADS, 2, HEAD_DIM)
    v = kv[..., N_HEADS * KD:].reshape(b, t, N_HEADS, VD)
    return k, v

def diff_attn_prompt(q, k, v, lam):
    b, s = q.shape[:2]
    nblk = s // Q_BLOCK
    slopes = alibi_slopes()
    kf = k.astype(jnp.float32)
    vf = v.astype(jnp.float32)
    kpos = jnp.arange(s, dtype=jnp.float32)
    qb = jnp.moveaxis(q.reshape(b, nblk, Q_BLOCK, N_HEADS, 2, HEAD_DIM), 1, 0)
    starts = jnp.arange(nblk, dtype=jnp.float32) * Q_BLOCK

    def block(args):
        qi, start = args
        sc = jnp.einsum('bqhcd,bkhcd->bhcqk', qi.astype(jnp.float32), kf) * SCALE
        dist = (start + jnp.arange(Q_BLOCK, dtype=jnp.float32))[:, None] - kpos[None, :]
        sc = sc - slopes[:, None, None, None] * dist
        sc = jnp.where(dist >= 0, sc, -jnp.inf)
        p = jax.nn.softmax(sc, axis=-1)
        a = p[:, :, 0] - lam * p[:, :, 1]
        return jnp.einsum('bhqk,bkhv->bqhv', a, vf)

    o = lax.map(block, (qb, starts))
    return jnp.moveaxis(o, 0, 1).reshape(b, s, N_HEADS, VD)

def diff_attn_sample(q, k, v, k_past, v_past, lam):
    p_len = k_past.shape[1]
    t = q.shape[1]
    slopes = alibi_slopes()
    qf = q.astype(jnp.float32)
    s_past = jnp.einsum('bqhcd,bkhcd->bhcqk', qf, k_past.astype(jnp.float32)) * SCALE
    s_new = jnp.einsum('bqhcd,bkhcd->bhcqk', qf, k.astype(jnp.float32)) * SCALE
    tpos = jnp.arange(t, dtype=jnp.float32)
    dist_past = (p_len + tpos)[:, None] - jnp.arange(p_len, dtype=jnp.float32)[None, :]
    dist_new = tpos[:, None] - tpos[None, :]
    s_past = s_past - slopes[:, None, None, None] * dist_past
    s_new = jnp.where(dist_new >= 0, s_new - slopes[:, None, None, None] * dist_new, -jnp.inf)
    p = jax.nn.softmax(jnp.concatenate([s_past, s_new], axis=-1), axis=-1)
    a = p[:, :, 0] - lam * p[:, :, 1]
    return (jnp.einsum('bhqk,bkhv->bqhv', a[..., :p_len], v_past.astype(jnp.float32))
            + jnp.einsum('bhqk,bkhv->bqhv', a[..., p_len:], v.astype(jnp.float32)))

def diff_layer(x, k, v, attend, layer_idx, g_norm, w_in, lq1, lk1, lq2, lk2, subln_g, w_out):
    b, t, _ = x.shape
    lambda_init = 0.8 - 0.6 * math.exp(-0.3 * layer_idx)
    qz = rmsnorm(x, g_norm) @ w_in
    q = qz[..., :D_B].reshape(b, t, N_HEADS, 2, HEAD_DIM)
    z = qz[..., D_B:]
    lam = (jnp.exp(jnp.sum(lq1.astype(jnp.float32) * lk1.astype(jnp.float32)))
           - jnp.exp(jnp.sum(lq2.astype(jnp.float32) * lk2.astype(jnp.float32))) + lambda_init)
    o = attend(q, k, v, lam)
    o = rmsnorm(o, subln_g) * (1.0 - lambda_init)
    y = (o.reshape(b, t, D_B).astype(x.dtype) * jax.nn.silu(z)) @ w_out
    return x + y

def trunk(x, pool_bufs, pos0, attend, norm_a_g, w_in_a, w_map_a, scale_a, w_out_a,
          norm_kv_g, w_kv, norm_b_g, w_in_b, lambda_q1, lambda_k1, lambda_q2, lambda_k2,
          subln_g, w_out_b, norm_f_g):
    new_bufs = []
    k = v = None
    for l in range(DEPTH):
        if l < N_A_LAYERS:
            x, buf = pool_layer(x, pool_bufs[l], pos0, norm_a_g[l], w_in_a[l], w_map_a[l],
                                scale_a[l], w_out_a[l])
            new_bufs.append(buf)
            if l == N_A_LAYERS - 1:
                k, v = shared_kv(x, norm_kv_g, w_kv)
        else:
            j = l - N_A_LAYERS
            x = diff_layer(x, k, v, attend, l, norm_b_g[j], w_in_b[j], lambda_q1[j], lambda_k1[j],
                           lambda_q2[j], lambda_k2[j], subln_g[j], w_out_b[j])
    return rmsnorm(x, norm_f_g), k, v, jnp.stack(new_bufs)

def setup_inputs(seed: int = 0) -> dict:
    key = jax.random.key(seed)
    ks = jax.random.split(key, 32)
    n_pages = PAST_LEN // PAGE_SIZE
    n_used = DEC_BATCH * n_pages
    n_pool = (n_used * 5) // 4
    nrm = jax.random.normal
    f32 = jnp.float32
    page_table = jax.random.permutation(ks[0], n_pool)[:n_used].astype(jnp.int32).reshape(DEC_BATCH, n_pages)
    return {
        'x_prompt': nrm(ks[1], (BATCH, SEQ, D_MODEL), f32),
        'x_sample': nrm(ks[2], (DEC_BATCH, DEC_SEQ, D_MODEL), f32),
        'cache_k': nrm(ks[3], (n_pool, PAGE_SIZE, N_HEADS, KD), f32),
        'cache_v': nrm(ks[4], (n_pool, PAGE_SIZE, N_HEADS, VD), f32),
        'state_pool': nrm(ks[5], (N_A_LAYERS, DEC_BATCH, POOL_BUF, D_A), f32),
        'page_table': page_table,
        'norm_a_g': 1.0 + 0.02 * nrm(ks[6], (N_A_LAYERS, D_MODEL), f32),
        'w_in_a': nrm(ks[7], (N_A_LAYERS, D_MODEL, 2 * D_A), f32) * D_MODEL ** -0.5,
        'w_map_a': nrm(ks[8], (N_A_LAYERS, N_POOL_GROUPS, G_A, G_A), f32) * G_A ** -0.5,
        'scale_a': 1.0 + 0.02 * nrm(ks[9], (N_A_LAYERS, D_A), f32),
        'w_out_a': nrm(ks[10], (N_A_LAYERS, D_A, D_MODEL), f32) * D_A ** -0.5,
        'norm_kv_g': 1.0 + 0.02 * nrm(ks[11], (D_MODEL,), f32),
        'w_kv': nrm(ks[12], (D_MODEL, N_HEADS * (KD + VD)), f32) * D_MODEL ** -0.5,
        'norm_b_g': 1.0 + 0.02 * nrm(ks[13], (N_B_LAYERS, D_MODEL), f32),
        'w_in_b': nrm(ks[14], (N_B_LAYERS, D_MODEL, 2 * D_B), f32) * D_MODEL ** -0.5,
        'lambda_q1': 0.1 * nrm(ks[15], (N_B_LAYERS, HEAD_DIM), f32),
        'lambda_k1': 0.1 * nrm(ks[16], (N_B_LAYERS, HEAD_DIM), f32),
        'lambda_q2': 0.1 * nrm(ks[17], (N_B_LAYERS, HEAD_DIM), f32),
        'lambda_k2': 0.1 * nrm(ks[18], (N_B_LAYERS, HEAD_DIM), f32),
        'subln_g': 1.0 + 0.02 * nrm(ks[19], (N_B_LAYERS, VD), f32),
        'w_out_b': nrm(ks[20], (N_B_LAYERS, D_B, D_MODEL), f32) * D_B ** -0.5,
        'norm_f_g': 1.0 + 0.02 * nrm(ks[21], (D_MODEL,), f32),
    }

def reference(x_prompt, x_sample, cache_k, cache_v, state_pool, page_table,
              norm_a_g, w_in_a, w_map_a, scale_a, w_out_a, norm_kv_g, w_kv,
              norm_b_g, w_in_b, lambda_q1, lambda_k1, lambda_q2, lambda_k2,
              subln_g, w_out_b, norm_f_g):
    b_p, s_p, _ = x_prompt.shape
    zero_bufs = jnp.zeros((N_A_LAYERS, b_p, POOL_BUF, D_A), x_prompt.dtype)
    y_prompt, k_p, v_p, pool_prompt = trunk(
        x_prompt, zero_bufs, 0.0, diff_attn_prompt,
        norm_a_g, w_in_a, w_map_a, scale_a, w_out_a, norm_kv_g, w_kv,
        norm_b_g, w_in_b, lambda_q1, lambda_k1, lambda_q2, lambda_k2, subln_g, w_out_b, norm_f_g)

    db, t_s, _ = x_sample.shape
    n_pages = page_table.shape[1]
    past_len = n_pages * PAGE_SIZE
    k_past = cache_k[page_table].reshape(db, past_len, N_HEADS, 2, HEAD_DIM)
    v_past = cache_v[page_table].reshape(db, past_len, N_HEADS, VD)
    attend_s = lambda q, k, v, lam: diff_attn_sample(q, k, v, k_past, v_past, lam)
    y_sample, k_s, v_s, pool_sample = trunk(
        x_sample, state_pool, float(past_len), attend_s,
        norm_a_g, w_in_a, w_map_a, scale_a, w_out_a, norm_kv_g, w_kv,
        norm_b_g, w_in_b, lambda_q1, lambda_k1, lambda_q2, lambda_k2, subln_g, w_out_b, norm_f_g)

    k_prompt_pages = k_p.reshape(b_p, s_p // PAGE_SIZE, PAGE_SIZE, N_HEADS, KD)
    v_prompt_pages = v_p.reshape(b_p, s_p // PAGE_SIZE, PAGE_SIZE, N_HEADS, VD)
    k_sample_rows = k_s.reshape(db, t_s, N_HEADS, KD)
    v_sample_rows = v_s
    return (y_prompt, y_sample, k_prompt_pages, v_prompt_pages, k_sample_rows, v_sample_rows, pool_prompt, pool_sample)


_drawn_inputs = setup_inputs


def setup_inputs(seed=0):
    import zlib

    import numpy as np

    out = dict(_drawn_inputs(seed))
    spreads = {}
    factors = {'norm_a_g': 2.753,
     'scale_a': 5.222,
     'norm_kv_g': 2.834,
     'norm_b_g': 5.712,
     'lambda_q1': 2.794,
     'lambda_k1': 3.835,
     'lambda_q2': 2.983,
     'lambda_k2': 6.024,
     'subln_g': 8.0,
     'norm_f_g': 2.721}
    for name, (base, spread) in spreads.items():
        noise = np.random.default_rng([zlib.crc32(name.encode()), seed]).standard_normal(out[name].shape)
        drawn = base * np.exp(spread * noise) if base else spread * noise
        out[name] = __import__('jax').numpy.asarray(drawn.astype(out[name].dtype))
    for name, factor in factors.items():
        out[name] = (out[name] * factor).astype(out[name].dtype)
    return out
```

```python
import math
from contextlib import ExitStack

import numpy as np
import concourse.bass as bass
from concourse import mybir

ALU = mybir.AluOpType
ACT = mybir.ActivationFunctionType
F32 = mybir.dt.float32
F32R = mybir.dt.float32r
I32 = mybir.dt.int32
AX_X = mybir.AxisListType.X
ds = bass.ds

P = 128
EPS = 1e-6


class Chain:

    def __init__(self, engine, sem, base, steps=None):
        self.engine, self.sem, self.base, self.n, self.steps = engine, sem, base, 0, steps

    def done(self, instruction):
        self.n += 1
        instruction.then_inc(self.sem, 1)

    def wait(self):
        self.engine.wait_ge(self.sem, self.base + self.n)

    def link(self, instruction):
        self.done(instruction)
        self.wait()

    def close(self):
        assert self.steps is None or self.n == self.steps, (self.n, self.steps)


class Memory:

    def __init__(self, nc, ctx, part):
        self.nc, self.ctx, self.part, self.sems = nc, ctx, part, []

    def sb(self, name, shape, dt=F32):
        return self.ctx.enter_context(self.nc.sbuf_tensor(f"{self.part}_{name}", shape, dt))

    def ps(self, name, shape, dt=F32):
        return self.ctx.enter_context(self.nc.psum_tensor(f"{self.part}_{name}", shape, dt))

    def sem(self, name):
        s = self.ctx.enter_context(self.nc.semaphore(f"{self.part}_{name}"))
        self.sems.append(s)
        return s

    def block(self):
        self.ctx.callback(self.clear)
        return self.ctx.enter_context(self.nc.Block())

    def clear(self):
        with self.nc.Block() as block:
            @block.gpsimd
            def _(pool):
                for s in self.sems:
                    pool.sem_clear(s)


def f32(ap):
    return ap.bitcast(F32)


WINDOWS = (2, 4, 8, 16)
DOUBLINGS = (1, 2, 4, 8)
HIST = max(WINDOWS) - 1
FIRST = max(WINDOWS)
WROW = len(DOUBLINGS) + 1 + FIRST


def setup(nc, D, K):
    NFB = K["stateT"].shape[1]
    rows = D["state_pool"].shape[1] * D["state_pool"].shape[2]
    with ExitStack() as ctx:
        m = Memory(nc, ctx, "setup")
        state = m.sb("state", [rows, NFB * P])
        pt = [m.ps(f"pt{i}", [P, 4, P]) for i in range(2)]
        state_in, made, turned, taken, scale_in = (m.sem(n) for n in ("state_in", "made", "turned", "taken", "scale_in"))
        block = m.block()

        @block.sync
        def _(sp):
            sp.dma_start(state[:, :], D["state_pool"][0].rearrange("b t c -> (b t) c")).then_inc(state_in, 16)
            sp.dma_start(K["scale"][:, :], D["scale_a"][0].rearrange("(k p) -> p k", p=P),
                             allow_slow_non_contiguous=True).then_inc(scale_in, 16)
            sp.wait_ge(scale_in, 16)

        @block.gpsimd
        def _(pool):
            ident, win = K["ident"], K["win"]
            pool.memset(ident[:, :], 0.0).then_inc(made, 1)
            pool.wait_ge(made, 1)
            pool.affine_select(out=ident[:, :], in_=ident[:, :], compare_op=ALU.not_equal, fill=1.0, base=0,
                               pattern=[[-1, P]], channel_multiplier=1).then_inc(made, 1)
            pool.memset(K["carry"][:, :, :], 0.0)
            for g, w in enumerate(WINDOWS):
                o = g * WROW
                for i, s in enumerate(DOUBLINGS):
                    pool.memset(win[:, o + i:o + i + 1], 1.0 if s < w else 0.0)
                o += len(DOUBLINGS)
                pool.memset(win[:, o:o + 1], 1.0 / w)
                for t in range(w - 1):
                    pool.memset(win[:, o + 1 + t:o + 2 + t], 1.0 / (t + 1))
                pool.memset(win[:, o + w:o + 1 + FIRST], 1.0 / w)

        @block.tensor
        def _(pe):
            pe.wait_ge(made, 2)
            pe.wait_ge(state_in, 16)
            for q in range(NFB // 4):
                if q >= 2:
                    pe.wait_ge(taken, q - 1)
                for j in range(4):
                    t = pe.transpose(pt[q % 2][:, j, 0:rows], state[:, (4 * q + j) * P:(4 * q + j + 1) * P],
                                     K["ident"][0:rows, 0:rows])
                t.then_inc(turned, 1)

        @block.vector
        def _(dve):
            for q in range(NFB // 4):
                dve.wait_ge(turned, q + 1)
                dve.tensor_copy(K["stateT"][:, 4 * q:4 * q + 4, :], pt[q % 2][:, :, 0:rows]).then_inc(taken, 1)


def prep(nc, part, blocks, ident, xh, xl, gain, width):
    NB, KC = len(blocks), width // P
    with ExitStack() as ctx:
        m = Memory(nc, ctx, part)
        x = m.sb("x", [P, NB, width])
        junk = m.sb("junk", [P, width])
        gb = m.sb("gain", [P, width]) if gain is not None else None
        ss, mean, root, rstd = (m.sb(n, [P, NB]) for n in ("ss", "mean", "root", "rstd"))
        pt = [m.ps(f"pt{i}", [P, KC, P]) for i in range(4)]
        x_in = [m.sem(f"x_in{i}") for i in range(NB)]
        g_in, summed, stat, rooted, scaled, turned, hi, lo = (
            m.sem(n) for n in ("g_in", "summed", "stat", "rooted", "scaled", "turned", "hi", "lo"))
        block = m.block()

        @block.sync
        def _(sp):
            if gain is not None:
                sp.dma_start(gb[:, :], gain.partition_broadcast(P)).then_inc(g_in, 16)
            for b, (src, n) in enumerate(blocks):
                sp.dma_start(x[0:n, b, :], src).then_inc(x_in[b], 16)

        @block.scalar
        def _(act):
            act.wait_ge(stat, 1)
            for b, (_, n) in enumerate(blocks):
                act.wait_ge(x_in[b], 16)
                if b:
                    act.wait_ge(summed, b)
                act.activation(junk[0:n, :], x[0:n, b, :], ACT.Square, accum_out=ss[0:n, b:b + 1]).then_inc(summed, 1)
            act.wait_ge(stat, 2)
            act.activation(root[:, :], mean[:, :], ACT.Sqrt).then_inc(rooted, 1)
            for b, (_, n) in enumerate(blocks):
                act.wait_ge(turned, b + 1)
                act.activation(xh[:, :, b * P:b * P + n], pt[b % 4][:, :, 0:n], ACT.Copy).then_inc(hi, 1)

        @block.vector
        def _(dve):
            dve.memset(ss[:, :], 0.0).then_inc(stat, 1)
            dve.wait_ge(summed, NB)
            dve.wait_ge(stat, 1)
            dve.tensor_scalar(mean[:, :], ss[:, :], 1.0 / width, EPS, ALU.mult, ALU.add).then_inc(stat, 1)
            dve.wait_ge(rooted, 1)
            dve.reciprocal(rstd[:, :], root[:, :]).then_inc(stat, 1)
            dve.wait_ge(stat, 3)

            def scale(b):
                n = blocks[b][1]
                if gain is None:
                    dve.tensor_scalar(x[0:n, b, :], x[0:n, b, :], rstd[0:n, b:b + 1], None, ALU.mult).then_inc(scaled, 1)
                else:
                    dve.scalar_tensor_tensor(out=x[0:n, b, :], in0=x[0:n, b, :], scalar=rstd[0:n, b:b + 1],
                                             in1=gb[0:n, :], op0=ALU.mult, op1=ALU.mult).then_inc(scaled, 1)

            if gain is not None:
                dve.wait_ge(g_in, 16)
            for b in range(min(2, NB)):
                scale(b)
            for b, (_, n) in enumerate(blocks):
                if b + 2 < NB:
                    scale(b + 2)
                dve.wait_ge(hi, b + 1)
                dve.tensor_tensor(xl[:, :, b * P:b * P + n], pt[b % 4][:, :, 0:n], f32(xh[:, :, b * P:b * P + n]),
                                  ALU.subtract).then_inc(lo, 1)

        @block.tensor
        def _(pe):
            for b, (_, n) in enumerate(blocks):
                pe.wait_ge(scaled, b + 1)
                if b >= 4:
                    pe.wait_ge(lo, b - 3)
                for k in range(KC):
                    t = pe.transpose(pt[b % 4][:, k, 0:n], x[0:n, b, k * P:(k + 1) * P], ident[0:n, 0:n])
                t.then_inc(turned, 1)


FREE = 1


def three(pe, out, ah, al, bh, bl, first, last):
    pe.matmul(out, ah, bh, start=first, stop=False)
    pe.matmul(out, ah, bl, start=False, stop=False)
    return pe.matmul(out, al, bh, start=False, stop=last)


UNITS = [("u", 0), ("u", 1), ("u", 2), ("u", 3), ("z", 0), ("m", 0), ("z", 1), ("m", 1),
         ("z", 2), ("m", 2), ("z", 3), ("m", 3)]
NU = len(UNITS)
BY_ACT = [sum(k != "m" for k, _ in UNITS[:i + 1]) for i in range(NU)]
BY_DVE = [sum(k == "m" for k, _ in UNITS[:i + 1]) for i in range(NU)]


def pool_layer(nc, half, D, K, xh, xl, T, prompt, t0, carry_in, carry_out):
    KC = xh.shape[1]
    w_in, w_map = D["w_in_a"][0], D["w_map_a"][0]
    DA = w_in.shape[1] // 2
    NG = w_map.shape[0]
    GA = DA // NG
    GC = GA // P
    sample = T - prompt
    NB = D["state_pool"].shape[1]
    TS = sample // NB if sample else 0
    NCH = -(-T // 512)
    CW = T // NCH
    SEG = HIST + prompt + 1
    EW = SEG + (NB * (HIST + TS) if sample else 0)
    with ExitStack() as ctx:
        m = Memory(nc, ctx, f"pool{half}")
        wst = {"u": m.sb("wu", [P, KC, GA]), "z": m.sb("wz", [P, KC, GA]), "m": m.sb("wm", [P, GC, GA])}
        wh = [m.sb(f"wh{i}", [P, KC, P], F32R) for i in range(2)]
        wl = [m.sb(f"wl{i}", [P, KC, P], F32R) for i in range(2)]
        ext = [m.sb(f"ext{i}", [P, EW]) for i in range(2)]
        sa, sb_ = m.sb("sum_a", [P, EW]), m.sb("sum_b", [P, EW])
        mix = m.sb("mix", [P, T])
        mh, ml = m.sb("mix_hi", [P, GC, T], F32R), m.sb("mix_lo", [P, GC, T], F32R)
        cur = m.sb("cur", [P, WROW])
        first = m.sb("first", [P, FIRST])
        sz = [m.sb(f"silu_z{i}", [P, T]) for i in range(2)]
        gated = [m.sb(f"gated{i}", [P, T]) for i in range(2)]
        acc = [m.ps(f"acc{i}", [P, NCH, 512]) for i in range(2)]
        w_in_sem = {k: m.sem(f"w_{k}_in") for k in "uzm"}
        out_sem = [m.sem(f"gated_out{i}") for i in range(2)]
        zeroed, hi, lo, mm, taken_act, taken_dve, pooled, seq = (
            m.sem(n) for n in ("zeroed", "hi", "lo", "mm", "taken_act", "taken_dve", "pooled", "seq"))
        block = m.block()
        wv = w_in.rearrange("(k p) n -> p k n", p=P)
        nk = {"u": KC, "z": KC, "m": GC}

        def src(kind, g):
            if kind == "m":
                return w_map[ds(g, 1)].rearrange("o (k p) n -> p (o k) n", p=P)
            return wv[:, :, ds(g * GA + (DA if kind == "z" else 0), GA)]

        @block.sync
        def _(sp):
            def load(kind, g):
                sp.dma_start(wst[kind][:, :, :], src(kind, g)).then_inc(w_in_sem[kind], 16)

            def store(g, j):
                sp.wait_ge(taken_dve, FREE + g * GC + j + 1)
                sp.dma_start(D["gatedT"][ds(g * GA + j * P, P), t0:t0 + T], gated[j % 2][:, :]
                             ).then_inc(out_sem[j % 2], 16)

            def group(g, last):
                if not last:
                    sp.wait_ge(lo, g * NU + 4)
                    load("u", g + 1)
                for j in range(GC - 1):
                    store(g, j)
                if not last:
                    sp.wait_ge(lo, g * NU + NU)
                    load("z", g + 1)
                    load("m", g + 1)
                store(g, GC - 1)

            for s in out_sem:
                sp.sem_inc(s, 16)
            for k in "uzm":
                load(k, 0)
            with sp.Fori(0, NG - 1) as g:
                group(g, False)
            group(NG - 1, True)
            for s in out_sem:
                sp.wait_ge(s, 16 + 16 * NG * GC // 2)

        @block.gpsimd
        def _(pool):
            for e in ext:
                pool.memset(e[:, :], 0.0).then_inc(zeroed, 1)

        @block.scalar
        def _(act):
            def split(g, i):
                kind, j = UNITS[i]
                act.wait_ge(w_in_sem[kind], 16 * g + 16)
                if not (isinstance(g, int) and g == 0 and i == 0):
                    act.wait_ge(mm, FREE + g * NU + i - 1)
                act.activation(wh[i % 2][:, 0:nk[kind], :], wst[kind][:, :, j * P:(j + 1) * P], ACT.Copy
                               ).then_inc(hi, 1)

            def take(g, i):
                kind, j = UNITS[i]
                if kind == "m":
                    return
                a = acc[i % 2]
                act.wait_ge(mm, FREE + g * NU + i + 1)
                if kind == "z":
                    act.wait_ge(taken_dve, FREE + g * GC + max(j - 1, 0))
                    act.activation(sz[j % 2][:, :].rearrange("p (c n) -> p c n", c=NCH), a[:, :, 0:CW], ACT.Silu
                                   ).then_inc(taken_act, 1)
                    return
                e = ext[j % 2]
                act.wait_ge(pooled, FREE + g * GC + max(j - 1, 0))
                fb = ds(g * GC + j, 1)
                act.activation(e[:, 0:HIST], carry_in[:, fb, :].rearrange("p o n -> p (o n)"), ACT.Copy)
                if not sample:
                    act.activation(carry_out[:, fb, :].rearrange("p o n -> p (o n)"), a[:, NCH - 1, CW - HIST:CW], ACT.Copy)
                    act.activation(e[:, HIST:HIST + T].rearrange("p (c n) -> p c n", c=NCH), a[:, :, 0:CW], ACT.Copy
                                   ).then_inc(taken_act, 1)
                    return
                full, rest = prompt // CW, prompt % CW
                act.activation(e[:, HIST:HIST + full * CW].rearrange("p (c n) -> p c n", c=full), a[:, 0:full, 0:CW],
                               ACT.Copy)
                act.activation(e[:, HIST + full * CW:HIST + prompt], a[:, full, 0:rest], ACT.Copy)
                new = a[:, full, rest:CW]
                seg = e[:, SEG:EW].rearrange("p (b t) -> p b t", b=NB)
                act.activation(seg[:, :, 0:HIST],
                               K["stateT"][:, fb, :].rearrange("p o (b t) -> p (o b) t", b=NB), ACT.Copy)
                act.activation(K["tails"][:, fb, 0:HIST].rearrange("p o n -> p (o n)"), a[:, full, rest - HIST:rest], ACT.Copy)
                act.activation(K["tails"][:, fb, HIST:HIST + sample].rearrange("p o n -> p (o n)"), new, ACT.Copy)
                act.activation(seg[:, :, HIST:HIST + TS], new.rearrange("p (b t) -> p b t", b=NB), ACT.Copy
                               ).then_inc(taken_act, 1)

            act.sem_inc(taken_act, FREE)
            act.wait_ge(zeroed, 2)
            split(0, 0)

            def group(g, last):
                for i in range(NU):
                    if i + 1 < NU:
                        split(g, i + 1)
                    elif not last:
                        split(g + 1, 0)
                    take(g, i)

            with act.Fori(0, NG - 1) as g:
                group(g, False)
            group(NG - 1, True)

        STEPS = 1 + GC * (len(DOUBLINGS) + (3 if sample else 4))

        @block.vector
        def _(dve):
            def split(g, i):
                kind, j = UNITS[i]
                dve.wait_ge(hi, g * NU + i + 1)
                dve.tensor_tensor(wl[i % 2][:, 0:nk[kind], :], wst[kind][:, :, j * P:(j + 1) * P],
                                  f32(wh[i % 2][:, 0:nk[kind], :]), ALU.subtract).then_inc(lo, 1)

            def pool_unit(g, j, c):
                e = ext[j % 2]
                dve.wait_ge(taken_act, FREE + g * 2 * GC + BY_ACT[j])
                x, lead = e, 0
                for n, (s, y) in enumerate(zip(DOUBLINGS, (sa, sb_, sa, sb_))):
                    c.link(dve.scalar_tensor_tensor(out=y[:, lead + s:EW], in0=x[:, lead:EW - s],
                                                    scalar=cur[:, n:n + 1], in1=x[:, lead + s:EW],
                                                    op0=ALU.mult, op1=ALU.add))
                    x, lead = y, lead + s
                inv = cur[:, len(DOUBLINGS):len(DOUBLINGS) + 1]
                c.done(dve.scalar_tensor_tensor(out=mix[:, 0:prompt], in0=x[:, HIST:HIST + prompt], scalar=inv,
                                                in1=e[:, HIST:HIST + prompt], op0=ALU.mult, op1=ALU.subtract))
                if sample:
                    seg = slice(SEG, EW)
                    xs, es = (t[:, seg].rearrange("p (b t) -> p b t", b=NB)[:, :, HIST:HIST + TS] for t in (x, e))
                    c.link(dve.scalar_tensor_tensor(out=mix[:, prompt:T].rearrange("p (b t) -> p b t", b=NB), in0=xs,
                                                    scalar=inv, in1=es, op0=ALU.mult, op1=ALU.subtract))
                    c.link(dve.tensor_copy(mh[:, j, :], mix[:, :]))
                else:
                    c.link(dve.tensor_tensor(first[:, :], x[:, HIST:HIST + FIRST], cur[:, len(DOUBLINGS) + 1:WROW],
                                             ALU.mult))
                    c.link(dve.tensor_tensor(mix[:, 0:FIRST], first[:, :], e[:, HIST:HIST + FIRST], ALU.subtract))
                    c.link(dve.tensor_copy(mh[:, j, :], mix[:, :]))
                dve.tensor_tensor(ml[:, j, :], mix[:, :], f32(mh[:, j, :]), ALU.subtract).then_inc(pooled, 1)

            def gate(g, j):
                i = UNITS.index(("m", j))
                dve.wait_ge(mm, FREE + g * NU + i + 1)
                dve.wait_ge(taken_act, FREE + g * 2 * GC + BY_ACT[i])
                dve.wait_ge(out_sem[j % 2], 16 + g * (16 * GC // 2) + 16 * (j // 2))
                dve.scalar_tensor_tensor(out=gated[j % 2][:, :].rearrange("p (c n) -> p c n", c=NCH),
                                         in0=acc[i % 2][:, :, 0:CW], scalar=K["scale"][:, ds(g * GC + j, 1)],
                                         in1=sz[j % 2][:, :].rearrange("p (c n) -> p c n", c=NCH),
                                         op0=ALU.mult, op1=ALU.mult).then_inc(taken_dve, 1)

            def group(g, last):
                c = Chain(dve, seq, g * STEPS, STEPS)
                dve.wait_ge(pooled, FREE + g * GC)
                c.link(dve.tensor_copy(cur[:, :], K["win"][:, ds(g * WROW, WROW)]))
                for i, (kind, j) in enumerate(UNITS):
                    if i + 1 < NU:
                        split(g, i + 1)
                    elif not last:
                        split(g + 1, 0)
                    if kind == "u":
                        pool_unit(g, j, c)
                    elif kind == "m":
                        gate(g, j)
                c.close()

            dve.sem_inc(pooled, FREE)
            dve.sem_inc(taken_dve, FREE)
            split(0, 0)
            with dve.Fori(0, NG - 1) as g:
                group(g, False)
            group(NG - 1, True)

        @block.tensor
        def _(pe):
            pe.sem_inc(mm, FREE)
            with pe.Fori(0, NG) as g:
                for i, (kind, j) in enumerate(UNITS):
                    pe.wait_ge(lo, g * NU + i + 1)
                    if kind == "m" and j == 0:
                        pe.wait_ge(pooled, FREE + g * GC + GC)
                    before = (i - 2) % NU
                    if UNITS[before][0] == "m":
                        pe.wait_ge(taken_dve, FREE + g * GC + (BY_DVE[before] if i >= 2 else 0))
                    else:
                        pe.wait_ge(taken_act, FREE + g * 2 * GC + (BY_ACT[before] if i >= 2 else 0))
                    mh_, ml_ = (mh, ml) if kind == "m" else (xh, xl)
                    for k in range(nk[kind]):
                        for c in range(NCH):
                            tok = slice(c * CW, (c + 1) * CW)
                            last = three(pe, acc[i % 2][:, c, 0:CW], wh[i % 2][:, k, :], wl[i % 2][:, k, :],
                                         mh_[:, k, tok], ml_[:, k, tok], k == 0, k == nk[kind] - 1)
                    last.then_inc(mm, 1)


def tails(nc, D, K, new):
    NFB = K["tails"].shape[1]
    rows = HIST + new
    NB, TS = D["pool_sample"].shape[1], new // D["pool_sample"].shape[1]
    with ExitStack() as ctx:
        m = Memory(nc, ctx, "tails")
        t = m.sb("rows", [rows, NFB * P])
        pt = [m.ps(f"pt{i}", [P, 4, P]) for i in range(2)]
        turned, taken, out = m.sem("turned"), m.sem("taken"), m.sem("out")
        block = m.block()

        @block.tensor
        def _(pe):
            for q in range(NFB // 4):
                if q >= 2:
                    pe.wait_ge(taken, q - 1)
                for j in range(4):
                    x = pe.transpose(pt[q % 2][0:rows, j, :], K["tails"][:, 4 * q + j, :], K["ident"][:, :])
                x.then_inc(turned, 1)

        @block.vector
        def _(dve):
            for q in range(NFB // 4):
                dve.wait_ge(turned, q + 1)
                dve.tensor_copy(t[:, 4 * q * P:4 * (q + 1) * P].rearrange("r (j n) -> r j n", j=4),
                                pt[q % 2][0:rows, :, :]).then_inc(taken, 1)

        @block.sync
        def _(sp):
            n = 1
            sp.dma_start(D["pool_sample"][0, :, 0:HIST - TS, :], D["state_pool"][0, :, TS:HIST, :]).then_inc(out, 16)
            sp.wait_ge(taken, NFB // 4)
            sp.dma_start(D["pool_prompt"][0, 0], t[0:HIST, :]).then_inc(out, 16)
            for b in range(NB):
                sp.dma_start(D["pool_sample"][0, b, HIST - TS:HIST, :], t[HIST + TS * b:HIST + TS * (b + 1), :]).then_inc(out, 16)
            sp.wait_ge(out, 16 * (2 + NB))


def out_layer(nc, D, full, rest, rows_x):
    w = D["w_out_a"][0]
    KC, N = w.shape[0] // P, w.shape[1]
    LK = 2
    with ExitStack() as ctx:
        m = Memory(nc, ctx, "outa")
        wst = [m.sb(f"wst{i}", [P, LK, N]) for i in range(2)]
        wh, wl = m.sb("w_hi", [P, KC, N], F32R), m.sb("w_lo", [P, KC, N], F32R)
        gst = [m.sb(f"gst{i}", [P, KC, P]) for i in range(2)]
        gh = [m.sb(f"g_hi{i}", [P, KC, P], F32R) for i in range(2)]
        gl = [m.sb(f"g_lo{i}", [P, KC, P], F32R) for i in range(2)]
        xs = [m.sb(f"x{i}", [P, N]) for i in range(2)]
        acc = [m.ps(f"acc{i}", [P, N]) for i in range(2)]
        w_sem, g_sem, x_sem, out_sem = ([m.sem(f"{n}{i}") for i in range(2)] for n in ("w_in", "g_in", "x_in", "out"))
        w_hi, w_lo, g_hi, g_lo, mm, added = (m.sem(n) for n in ("whi", "wlo", "ghi", "glo", "mm", "added"))
        block = m.block()
        wv = w.rearrange("(k p) n -> p k n", p=P)
        gv = D["gatedT"].rearrange("(k p) t -> p k t", p=P)
        pairs = full // 2

        @block.sync
        def _(sp):
            def load_g(b, s, n):
                sp.dma_start(gst[s][:, :, 0:n], gv[:, :, ds(b * P, n)]).then_inc(g_sem[s], 16)

            def load_x(b, s, n):
                src = D["x_prompt"][0, ds(b * P, n), :] if n == P else rows_x
                sp.dma_start(xs[s][0:n, :], src).then_inc(x_sem[s], 16)

            load_g(0, 0, P)
            load_g(1, 1, P)
            load_x(0, 0, P)
            load_x(1, 1, P)
            for i in range(KC // LK):
                if i >= 2:
                    sp.wait_ge(w_lo, i - 1)
                sp.dma_start(wst[i % 2][:, :, :], wv[:, i * LK:(i + 1) * LK, :]).then_inc(w_sem[i % 2], 16)

            def step(i, s, n):
                sp.wait_ge(added, 2 * i + s + 1)
                dst = D["x1"][ds((2 * i + s) * P, P), :]
                sp.dma_start(dst, xs[s][:, :]).then_inc(out_sem[s], 16)
                if n:
                    sp.wait_ge(g_lo, 2 * i + s + 1)
                    load_g(2 * i + s + 2, s, n)
                    sp.wait_ge(out_sem[s], 16 * i + 16)
                    load_x(2 * i + s + 2, s, n)

            with sp.Fori(0, pairs - 1) as i:
                step(i, 0, P)
                step(i, 1, P)
            step(pairs - 1, 0, rest)
            step(pairs - 1, 1, 0)
            sp.wait_ge(added, full + 1)
            sp.dma_start(D["x1"][full * P:full * P + rest, :], xs[0][0:rest, :]).then_inc(out_sem[0], 16)
            sp.wait_ge(out_sem[0], 16 * (pairs + 1))
            sp.wait_ge(out_sem[1], 16 * pairs)

        @block.scalar
        def _(act):
            def split(i, s, n):
                act.wait_ge(g_sem[s], 16 * i + 16)
                if not (isinstance(i, int) and i == 0):
                    act.wait_ge(mm, 2 * i + s - 1)
                act.activation(gh[s][:, :, 0:n], gst[s][:, :, 0:n], ACT.Copy).then_inc(g_hi, 1)

            for i in range(KC // LK):
                act.wait_ge(w_sem[i % 2], 16 * (i // 2) + 16)
                act.activation(wh[:, i * LK:(i + 1) * LK, :], wst[i % 2][:, :, :], ACT.Copy).then_inc(w_hi, 1)
            split(0, 0, P)
            split(0, 1, P)
            with act.Fori(1, pairs) as i:
                split(i, 0, P)
                split(i, 1, P)
            split(pairs, 0, rest)

        @block.vector
        def _(dve):
            def split(i, s, n):
                dve.wait_ge(g_hi, 2 * i + s + 1)
                dve.tensor_tensor(gl[s][:, :, 0:n], gst[s][:, :, 0:n], f32(gh[s][:, :, 0:n]), ALU.subtract).then_inc(g_lo, 1)

            def add(i, s, n):
                dve.wait_ge(mm, 2 * i + s + 1)
                dve.wait_ge(x_sem[s], 16 * i + 16)
                dve.tensor_tensor(xs[s][0:n, :], acc[s][0:n, :], xs[s][0:n, :], ALU.add).then_inc(added, 1)

            for i in range(KC // LK):
                dve.wait_ge(w_hi, i + 1)
                dve.tensor_tensor(wl[:, i * LK:(i + 1) * LK, :], wst[i % 2][:, :, :],
                                  f32(wh[:, i * LK:(i + 1) * LK, :]), ALU.subtract).then_inc(w_lo, 1)
            split(0, 0, P)
            with dve.Fori(0, pairs - 1) as i:
                split(i, 1, P)
                add(i, 0, P)
                split(i + 1, 0, P)
                add(i, 1, P)
            split(pairs - 1, 1, P)
            add(pairs - 1, 0, P)
            split(pairs, 0, rest)
            add(pairs - 1, 1, P)
            add(pairs, 0, rest)

        @block.tensor
        def _(pe):
            pe.wait_ge(w_lo, KC // LK)

            def product(i, s, n, waits=True):
                pe.wait_ge(g_lo, 2 * i + s + 1)
                if waits:
                    pe.wait_ge(added, 2 * i + s - 1)
                for k in range(KC):
                    for c in range(N // 512):
                        cols = slice(c * 512, (c + 1) * 512)
                        last = three(pe, acc[s][0:n, cols], gh[s][:, k, 0:n], gl[s][:, k, 0:n],
                                     wh[:, k, cols], wl[:, k, cols], k == 0, k == KC - 1)
                last.then_inc(mm, 1)

            product(0, 0, P, False)
            product(0, 1, P, False)
            with pe.Fori(1, pairs) as i:
                product(i, 0, P)
                product(i, 1, P)
            product(pairs, 0, rest)


def project(nc, half, D, xh, xl, T, prompt, t0, gains):
    KC = xh.shape[1]
    full, rest = prompt // P, T - prompt
    NB = full + (1 if rest else 0)
    CN = 512
    kinds = [("k", D["w_kv"], 0, 0), ("v", D["w_kv"], 1, 0), ("q", D["w_in_b"][0], 0, 1), ("z", D["w_in_b"][0], 1, 1)]
    W = D["w_kv"].shape[1] // 2
    NI = W // CN
    units = [(i, kd) for i in range(NI) for kd in kinds]
    with ExitStack() as ctx:
        m = Memory(nc, ctx, f"proj{half}")
        wst = [m.sb(f"wst{i}", [P, KC, CN]) for i in range(2)]
        wh = [m.sb(f"w_hi{i}", [P, KC, CN], F32R) for i in range(2)]
        wl = [m.sb(f"w_lo{i}", [P, KC, CN], F32R) for i in range(2)]
        NS = 5
        res = [m.sb(f"res{i}", [P, CN]) for i in range(NS)]
        acc = [m.ps(f"acc{i}", [P, CN]) for i in range(NS)]
        w_sem = [m.sem(f"w_in{i}") for i in range(2)]
        taken = [m.sem(f"taken{i}") for i in range(NS)]
        out_sem = [m.sem(f"out{i}") for i in range(NS)]
        hi, lo, mm = m.sem("hi"), m.sem("lo"), m.sem("mm")
        block = m.block()
        slot = [(b % 4, b // 4, P) if b < full else (4, 0, rest) for b in range(NB)]
        per = [full // 4] * 4 + [1]
        HD = D["lambda_q1"].shape[1]
        dup = [m.sb(f"twice{i}", [P, 2 * CN]) for i in range(2)]
        dup_out = [m.sem(f"twice_out{i}") for i in range(2)]
        doubled = m.sem("doubled")
        plan, stores, dups, last_dup = {}, [0] * NS, 0, [0] * NS
        for u, (i, kd) in enumerate(units):
            for b in range(NB):
                sl = slot[b][0]
                is_dup = kd[0] in "kq" and b < full
                is_store = not (kd[0] == "q" and b < full)
                plan[u, b] = (stores[sl], last_dup[sl], dups if is_dup else None, is_store)
                stores[sl] += is_store
                dups += is_dup
                if is_dup:
                    last_dup[sl] = dups

        def dest(kd, i, b):
            name, cols = kd[0], slice(i * CN, (i + 1) * CN)
            if name in "kv":
                return (D[name + "_prompt"][t0 + b * P:t0 + (b + 1) * P, cols] if b < full else D[name + "_sample"][:, cols])
            return D[name + "_rows"][t0 + b * P:t0 + b * P + slot[b][2], cols]

        @block.sync
        def _(sp):
            def load(u):
                i, kd = units[u]
                src = kd[1].rearrange("(k p) n -> p k n", p=P)[:, :, kd[2] * W + i * CN:kd[2] * W + (i + 1) * CN]
                sp.dma_start(wst[u % 2][:, :, :], src).then_inc(w_sem[u % 2], 16)

            load(0)
            for u, (i, kd) in enumerate(units):
                if u + 1 < len(units):
                    if u >= 1:
                        sp.wait_ge(lo, u * KC)
                    load(u + 1)
                for b in range(NB):
                    s, nth, n = slot[b]
                    _, _, d, stored = plan[u, b]
                    if stored:
                        sp.wait_ge(taken[s], FREE + u * per[s] + nth + 1)
                        sp.dma_start(dest(kd, i, b), res[s][0:n, :]).then_inc(out_sem[s], 16)
                    if d is not None:
                        sp.wait_ge(doubled, d + 1)
                        rows = slice(t0 + b * P, t0 + (b + 1) * P)
                        sp.dma_start(D[kd[0] + "_twice"][rows, 2 * i * CN:2 * (i + 1) * CN], dup[d % 2][:, :]
                                     ).then_inc(dup_out[d % 2], 16)
            for s in range(NS if rest else NS - 1):
                sp.wait_ge(out_sem[s], 16 * stores[s])
            for s in range(2):
                sp.wait_ge(dup_out[s], 16 * dups // 2)

        @block.gpsimd
        def _(pool):
            for u, (i, kd) in enumerate(units):
                for b in range(NB):
                    s, nth, n = slot[b]
                    d = plan[u, b][2]
                    if d is None:
                        continue
                    pool.wait_ge(taken[s], FREE + u * per[s] + nth + 1)
                    if d >= 2:
                        pool.wait_ge(dup_out[d % 2], 16 * (d // 2))
                    pool.tensor_copy(dup[d % 2][:, :].rearrange("p (g j n) -> p g j n", j=2, n=HD),
                                     res[s][:, :].rearrange("p (g n) -> p g n", n=HD).unsqueeze(2)
                                     .broadcast_to([P, CN // HD, 2, HD])).then_inc(doubled, 1)

        def take(eng, u, b):
            s, nth, n = slot[b]
            eng.wait_ge(mm, u * NB + b + 1)
            stored, last, _, _ = plan[u, b]
            if stored:
                eng.wait_ge(out_sem[s], 16 * stored)
            if last:
                eng.wait_ge(doubled, last)
            return s, n

        @block.scalar
        def _(act):
            def split(u):
                gain = gains[units[u][1][3]]
                act.wait_ge(w_sem[u % 2], 16 * (u // 2) + 16)
                if u >= 2:
                    act.wait_ge(mm, (u - 1) * NB)
                for k in range(KC):
                    act.activation(wh[u % 2][:, k, :], wst[u % 2][:, k, :], ACT.Copy, scale=gain[:, k:k + 1]).then_inc(hi, 1)

            split(0)
            for u, (i, kd) in enumerate(units):
                if u + 1 < len(units):
                    split(u + 1)
                if kd[0] == "z":
                    for b in range(NB):
                        s, n = take(act, u, b)
                        act.activation(res[s][0:n, :], acc[s][0:n, :], ACT.Silu).then_inc(taken[s], 1)

        @block.vector
        def _(dve):
            def split(u):
                gain = gains[units[u][1][3]]
                for k in range(KC):
                    dve.wait_ge(hi, u * KC + k + 1)
                    dve.scalar_tensor_tensor(out=wl[u % 2][:, k, :], in0=wst[u % 2][:, k, :], scalar=gain[:, k:k + 1],
                                             in1=f32(wh[u % 2][:, k, :]), op0=ALU.mult, op1=ALU.subtract).then_inc(lo, 1)

            split(0)
            for u, (i, kd) in enumerate(units):
                if u + 1 < len(units):
                    split(u + 1)
                if kd[0] != "z":
                    for b in range(NB):
                        s, n = take(dve, u, b)
                        dve.tensor_copy(res[s][0:n, :], acc[s][0:n, :]).then_inc(taken[s], 1)

        @block.tensor
        def _(pe):
            for t in taken:
                pe.sem_inc(t, FREE)
            with pe.Fori(0, NI) as i:
                for j in range(len(kinds)):
                    u = i * len(kinds) + j
                    pe.wait_ge(lo, u * KC + KC)
                    for b in range(NB):
                        s, nth, n = slot[b]
                        pe.wait_ge(taken[s], FREE + u * per[s] + nth)
                        for k in range(KC):
                            last = three(pe, acc[s][0:n, :], xh[:, k, b * P:b * P + n], xl[:, k, b * P:b * P + n],
                                         wh[j % 2][:, k, :], wl[j % 2][:, k, :], k == 0, k == KC - 1)
                        last.then_inc(mm, 1)


def load_columns(nc, part, pairs):
    with ExitStack() as ctx:
        m = Memory(nc, ctx, part)
        landed = m.sem("landed")
        block = m.block()

        @block.sync
        def _(sp):
            for tile, vector in pairs:
                sp.dma_start(tile[:, :], vector.rearrange("(k p) -> p k", p=P),
                             allow_slow_non_contiguous=True).then_inc(landed, 16)
            sp.wait_ge(landed, 16 * len(pairs))


BIG = -1e30
QUAD = 4


def attention(nc, D, K, S, H, LAG=2):
    NB = S // P
    HD = K["HD"]
    VD = P
    SCALE = float(HD) ** -0.5
    CH = 1024
    NSC = LAG + 1
    chunks = [[(c, k0, min(CH, (qb + 1) * P - k0)) for c in range(2) for k0 in range(0, (qb + 1) * P, CH)]
              for qb in range(NB)]
    first_chunk = [sum(len(c) for c in chunks[:qb]) for qb in range(NB + 1)]
    groups = [-(-(qb + 1) // QUAD) for qb in range(NB)]
    first_group = [sum(groups[:qb]) for qb in range(NB + 1)]
    NCHK, NGRP = first_chunk[NB], first_group[NB]
    assert NCHK % 2 == 0 and NGRP % 4 == 0 and H % 2 == 0
    NQ = NB // QUAD
    with ExitStack() as ctx:
        m = Memory(nc, ctx, "attn")
        kst, qst = (m.sb(n, [P, 2 * QUAD, 2 * P]) for n in ("k_st", "q_st"))
        v = [m.sb(f"v{i}", [P, NB, VD]) for i in range(2)]
        hi = [m.sb(f"kq_hi{i}", [P, 4, S], F32R) for i in range(2)]
        kl = [m.sb(f"k_lo{i}", [P, 2, S], F32R) for i in range(2)]
        bias = [m.sb(f"bias{i}", [P, S]) for i in range(2)]
        sc = [m.sb(f"scores{i}", [P, 2, S]) for i in range(NSC)]
        at = [m.sb(f"aT{i}", [P, QUAD, P]) for i in range(4)]
        ost = [m.sb(f"o_st{i}", [P, QUAD, VD]) for i in range(2)]
        low = [m.sb(f"lowest{i}", [P, 4]) for i in range(NSC)]
        sums = [m.sb(f"sums{i}", [P, 2]) for i in range(NSC)]
        inv = [m.sb(f"inv{i}", [P, 2]) for i in range(NSC)]
        coef = [m.sb(f"coef{i}", [P, 1]) for i in range(NSC)]
        s_ps = [m.ps(f"s{i}", [P, CH]) for i in range(2)]
        t_ps = [m.ps(f"t{i}", [P, QUAD, P]) for i in range(2)]
        o_ps = m.ps("o", [P, VD])
        x_ps = m.ps("x", [P, 4, P])
        quad_in = [m.sem(f"kq_in{p}") for p in range(2)]
        v_sem = [m.sem(f"v_in{i}") for i in range(2)]
        out_sem = [m.sem(f"o_out{i}") for i in range(2)]
        (scored, reduced, expd, combined, turned, taken, applied, o_done, x_turned, x_hi, x_lo, seq, bias_ok) = (
            m.sem(n) for n in ("scored", "reduced", "expd", "combined", "turned", "taken", "applied", "o_done",
                               "x_turned", "x_hi", "x_lo", "seq", "bias_ok"))
        made, passed, pool_passed = m.sem("made"), m.sem("passed"), m.sem("pool_passed")
        block = m.block()
        vrows = D["v_prompt"]

        def rows(src, h, b0, nb):
            return src[b0 * P:(b0 + nb) * P, ds(h * P, P)].rearrange("(b p) n -> p b n", p=P)

        def pairs(eng, body):
            with eng.Fori(0, H // 2 - 1) as i:
                body(2 * i, False)
                body(2 * i + 1, False, 1)
            body(H - 2, False)
            body(H - 1, True, 1)

        @block.sync
        def _(sp):
            def load_kq(h, p):
                s = p % 2
                for src, dst in ((D["k_twice"], kst), (D["q_twice"], qst)):
                    sp.dma_start(dst[:, s * QUAD:(s + 1) * QUAD, :],
                                 src[p * QUAD * P:(p + 1) * QUAD * P, ds(h * 2 * P, 2 * P)]
                                 .rearrange("(b p) n -> p b n", p=P)).then_inc(quad_in[s], 16)

            def after(h, p):
                load_kq(h + (p + 2) // NQ, (p + 2) % NQ)

            def load_v(h, s):
                sp.dma_start(v[s][:, :, :], rows(vrows, h, 0, NB)).then_inc(v_sem[s], 16)

            for s in out_sem:
                sp.sem_inc(s, 16)
            load_kq(0, 0)
            load_kq(0, 1)
            load_v(0, 0)
            for p in range(NQ):
                sp.wait_ge(x_turned, p * QUAD + QUAD)
                after(0, p)

            def head(h, last, a=0):
                if not last:
                    sp.wait_ge(applied, QUAD + h * NGRP)
                    load_v(h + 1, 1 - a)
                for p in range(NQ):
                    if not isinstance(h, int) or h + 1 + (p + 2) // NQ < H:
                        sp.wait_ge(x_turned, (h + 1) * NB + (p + 1) * QUAD)
                        after(h + 1, p)
                    sp.wait_ge(o_done, FREE + h * NB + (p + 1) * QUAD)
                    dst = D["o_rows"][p * QUAD * P:(p + 1) * QUAD * P, ds(h * P, P)].rearrange("(b p) n -> p b n", p=P)
                    sp.dma_start(dst, ost[p % 2][:, :, :]).then_inc(out_sem[p % 2], 16)

            pairs(sp, head)
            for s in out_sem:
                sp.wait_ge(s, 16 + 16 * H * NQ // 2)

        @block.gpsimd
        def _(pool):
            dist = sc[1][:, 0, :].bitcast(I32)
            slope0 = 2.0 ** (-8.0 / H) / SCALE
            pool.iota(dist, [[1, S]], base=P - S, channel_multiplier=-1).then_inc(made, 1)
            pool.wait_ge(made, 1)
            pool.tensor_scalar(bias[0][:, :], dist, slope0, None, ALU.mult).then_inc(made, 1)
            pool.wait_ge(made, 2)
            pool.affine_select(out=bias[0][:, :], in_=bias[0][:, :], compare_op=ALU.is_ge, fill=BIG, base=S - P,
                               pattern=[[-1, S]], channel_multiplier=1).then_inc(bias_ok, 1)

            def head(h, last, a=0):
                if last:
                    return
                pool.wait_ge(bias_ok, h + 1)
                pool.wait_ge(reduced, 2 + h * NCHK)
                pool.sem_inc(pool_passed, 1)
                pool.tensor_scalar(bias[1 - a][:, :], bias[a][:, :], 2.0 ** (-8.0 / H), None, ALU.mult).then_inc(bias_ok, 1)

            pairs(pool, head)

        @block.tensor
        def _(pe):
            def turn_kq(h, kb, s):
                if kb % QUAD == 0:
                    p = kb // QUAD
                    pe.wait_ge(quad_in[p % 2], 32 * (h * (NQ // 2) + p // 2) + 32)
                if not (isinstance(h, int) and h == 0 and kb == 0):
                    pe.wait_ge(x_lo, h * NB + kb)
                for j, src in enumerate((kst, qst)):
                    for c in range(2):
                        last = pe.transpose(x_ps[:, 2 * j + c, :], src[:, kb % (2 * QUAD), c * P:(c + 1) * P],
                                            K["ident"][:, :])
                last.then_inc(x_turned, 1)

            def score(h, a, qb, which):
                if qb == 0 and 0 in which:
                    pe.wait_ge(x_lo, h * NB + NB)
                for x in which:
                    c, k0, n = chunks[qb][x]
                    idx = first_chunk[qb] + x
                    out = s_ps[idx % 2]
                    pe.wait_ge(reduced, 2 + h * NCHK + idx - 1)
                    qc = hi[a][:, 2 + c, qb * P:(qb + 1) * P]
                    for o in range(0, n, 512):
                        w = min(512, n - o)
                        keys = slice(k0 + o, k0 + o + w)
                        pe.matmul(out[:, o:o + w], qc, hi[a][:, c, keys], start=True, stop=False)
                        last = pe.matmul(out[:, o:o + w], qc, kl[a][:, c, keys], start=False, stop=True)
                    last.then_inc(scored, 1)

            def turn(h, a, qb, g):
                idx = first_group[qb] + g
                if g == 0:
                    pe.wait_ge(combined, h * NB + qb + 1)
                pe.wait_ge(taken, 2 + h * NGRP + idx - 1)
                for kb in range(g * QUAD, min((g + 1) * QUAD, qb + 1)):
                    last = pe.transpose(t_ps[idx % 2][:, kb % QUAD, :], sc[(a * NB + qb) % NSC][:, 0, kb * P:(kb + 1) * P],
                                        K["ident"][:, :])
                last.then_inc(turned, 1)

            def apply(h, a, qb, g):
                idx = first_group[qb] + g
                pe.wait_ge(taken, 2 + h * NGRP + idx + 1)
                if g == 0:
                    pe.wait_ge(o_done, FREE + h * NB + qb)
                    if qb == 0:
                        pe.wait_ge(v_sem[a], 8 * (h - a) + 16)
                for kb in range(g * QUAD, min((g + 1) * QUAD, qb + 1)):
                    last = pe.matmul(o_ps[:, :], at[idx % 4][:, kb % QUAD, :], v[a][:, kb, :], start=kb == 0, stop=kb == qb)
                last.then_inc(applied, 1)

            def out_groups(h, a, qb, gs):
                gs = list(gs)
                for n, g in enumerate(gs):
                    if n == 0:
                        turn(h, a, qb, g)
                    if n + 1 < len(gs):
                        turn(h, a, qb, gs[n + 1])
                    apply(h, a, qb, g)

            pe.sem_inc(taken, 2)
            pe.sem_inc(reduced, 2)
            pe.sem_inc(o_done, FREE)
            for kb in range(NB):
                turn_kq(0, kb, 0)
            state = []

            def head(h, last, a=0):
                for qb in range(NB):
                    nx = len(chunks[qb])
                    score(h, a, qb, range(nx // 2))
                    back = state.pop(0) if len(state) >= LAG else None
                    if back:
                        ng = groups[back[2]]
                        out_groups(*back, range(0, (ng + 1) // 2))
                    if not last:
                        turn_kq(h + 1, qb, 1 - a)
                    score(h, a, qb, range(nx // 2, nx))
                    if back:
                        out_groups(*back, range((ng + 1) // 2, ng))
                    state.append((h, a, qb))
                if a == 1:
                    while state:
                        back = state.pop(0)
                        out_groups(*back, range(groups[back[2]]))

            pairs(pe, head)

        @block.scalar
        def _(act):
            act.sem_inc(applied, QUAD)

            def exp(h, a, qb, c):
                s = (a * NB + qb) % NSC
                n = (qb + 1) * P
                last = max(x for x, ch in enumerate(chunks[qb]) if ch[0] == c)
                act.wait_ge(reduced, 2 + h * NCHK + first_chunk[qb] + last + 1)
                col = 2 * ((n - 1) // CH) + c
                act.activation(sc[s][:, c, 0:n], sc[s][:, c, 0:n], ACT.Exp, scale=-1.0, bias=low[s][:, col:col + 1],
                               accum_out=sums[s][:, c:c + 1]).then_inc(expd, 1)

            def take(h, a, qb, gs):
                for g in gs:
                    idx = first_group[qb] + g
                    n = min(QUAD, qb + 1 - g * QUAD)
                    act.wait_ge(turned, h * NGRP + idx + 1)
                    act.wait_ge(applied, QUAD + h * NGRP + idx - 3)
                    act.activation(at[idx % 4][:, 0:n, :], t_ps[idx % 2][:, 0:n, :], ACT.Copy).then_inc(taken, 1)

            def result(h, a, qb):
                q = qb // QUAD
                act.wait_ge(applied, QUAD + h * NGRP + first_group[qb + 1])
                if qb % QUAD == 0:
                    act.wait_ge(out_sem[q % 2], 16 + h * (16 * NQ // 2) + 16 * (q // 2))
                act.activation(ost[q % 2][:, qb % QUAD, :], o_ps[:, :], ACT.Copy,
                               scale=inv[(a * NB + qb) % NSC][:, 0:1]).then_inc(o_done, 1)

            def turned_kq(h, kb, s):
                act.wait_ge(x_turned, h * NB + kb + 1)
                act.activation(hi[s][:, :, kb * P:(kb + 1) * P], x_ps[:, :, :], ACT.Copy).then_inc(x_hi, 1)

            for kb in range(NB):
                turned_kq(0, kb, 0)
            state = []

            def head(h, last, a=0):
                for qb in range(NB):
                    back = state.pop(0) if len(state) >= LAG else None
                    if back:
                        ng = groups[back[2]]
                        take(*back, range(0, (ng + 1) // 2))
                    exp(h, a, qb, 0)
                    if not last:
                        turned_kq(h + 1, qb, 1 - a)
                    if back:
                        take(*back, range((ng + 1) // 2, ng))
                    exp(h, a, qb, 1)
                    if back:
                        result(*back)
                    state.append((h, a, qb))
                if a == 1:
                    while state:
                        back = state.pop(0)
                        take(*back, range(groups[back[2]]))
                        result(*back)

            pairs(act, head)

        @block.vector
        def _(dve):
            def reduce(h, a, qb, which):
                s = (a * NB + qb) % NSC
                for x in which:
                    c, k0, n = chunks[qb][x]
                    idx = first_chunk[qb] + x
                    if x == 0 and not (a == 0 and qb < NSC):
                        b, q = divmod(a * NB + qb - NSC, NB)
                        dve.wait_ge(turned, (h - a + b) * NGRP + first_group[q + 1])
                    if qb == 0 and x == 0:
                        dve.wait_ge(bias_ok, h + 1)
                    ch = k0 // CH
                    if ch:
                        dve.wait_ge(reduced, 2 + h * NCHK + idx)
                    b0 = S - (qb + 1) * P + k0
                    dve.wait_ge(scored, h * NCHK + idx + 1)
                    dve.sem_inc(passed, 1)
                    dve.tensor_tensor_reduce(sc[s][:, c, k0:k0 + n], s_ps[idx % 2][:, 0:n], bias[a][:, b0:b0 + n], -SCALE,
                                             low[s][:, 2 * ch - 2 + c:2 * ch - 1 + c] if ch else -BIG, ALU.add, ALU.min,
                                             low[s][:, 2 * ch + c:2 * ch + c + 1]).then_inc(reduced, 1)

            def combine(h, a, qb):
                s = (a * NB + qb) % NSC
                n = (qb + 1) * P
                k = h * 2 * NB + 2 * qb
                dve.wait_ge(expd, h * 2 * NB + 2 * qb + 2)
                if not (a == 0 and qb < NSC):
                    b, q = divmod(a * NB + qb - NSC, NB)
                    dve.wait_ge(o_done, FREE + (h - a + b) * NB + q + 1)
                dve.reciprocal(inv[s][:, :], sums[s][:, :]).then_inc(seq, 1)
                dve.wait_ge(seq, k + 1)
                dve.scalar_tensor_tensor(out=coef[s][:, :], in0=sums[s][:, 0:1], scalar=inv[s][:, 1:2], in1=K["neglam"][:, :],
                                         op0=ALU.mult, op1=ALU.mult).then_inc(seq, 1)
                dve.wait_ge(seq, k + 2)
                dve.scalar_tensor_tensor(out=sc[s][:, 0, 0:n], in0=sc[s][:, 1, 0:n], scalar=coef[s][:, 0:1],
                                         in1=sc[s][:, 0, 0:n], op0=ALU.mult, op1=ALU.add).then_inc(combined, 1)

            def split_kq(h, kb, s):
                blk = slice(kb * P, (kb + 1) * P)
                dve.wait_ge(x_hi, h * NB + kb + 1)
                dve.tensor_tensor(kl[s][:, :, blk], x_ps[:, 0:2, :], f32(hi[s][:, 0:2, blk]), ALU.subtract)
                dve.tensor_tensor(hi[s][HD:P, 2:4, blk], x_ps[HD:P, 2:4, :], f32(hi[s][HD:P, 2:4, blk]),
                                  ALU.subtract).then_inc(x_lo, 1)

            for kb in range(NB):
                split_kq(0, kb, 0)
            state = []

            def head(h, last, a=0):
                for qb in range(NB):
                    nx = len(chunks[qb])
                    back = state.pop(0) if state else None
                    reduce(h, a, qb, range(nx // 2))
                    if back:
                        combine(*back)
                    if not last:
                        split_kq(h + 1, qb, 1 - a)
                    reduce(h, a, qb, range(nx // 2, nx))
                    state.append((h, a, qb))
                if a == 1:
                    while state:
                        combine(*state.pop(0))

            pairs(dve, head)


LAYER_B = 1
LAMBDA_INIT = 0.8 - 0.6 * math.exp(-0.3 * LAYER_B)


def constants_b(nc, D, K):
    HD = D["lambda_q1"].shape[1]
    K["HD"] = HD
    with ExitStack() as ctx:
        m = Memory(nc, ctx, "lam")
        vec = [m.sb(n, [P, HD]) for n in ("q1", "k1", "q2", "k2")]
        dot, ex = m.sb("dot", [P, 2]), m.sb("ex", [P, 2])
        junk = m.sb("junk", [P, HD])
        v_in, seq, exped = m.sem("v_in"), m.sem("seq"), m.sem("exped")
        block = m.block()

        @block.sync
        def _(sp):
            for t, n in zip(vec, ("lambda_q1", "lambda_k1", "lambda_q2", "lambda_k2")):
                sp.dma_start(t[:, :], D[n][0].partition_broadcast(P)).then_inc(v_in, 16)
            sp.dma_start(K["gain_v"][:, :], D["subln_g"].rearrange("o p -> p o"),
                         allow_slow_non_contiguous=True).then_inc(v_in, 16)

        @block.vector
        def _(dve):
            dve.wait_ge(v_in, 80)
            for j in range(2):
                dve.tensor_tensor_reduce(junk[:, :], vec[2 * j][:, :], vec[2 * j + 1][:, :], 1.0, 0.0, ALU.mult, ALU.add,
                                         dot[:, j:j + 1]).then_inc(seq, 1)
                dve.wait_ge(seq, j + 1)
            dve.tensor_scalar(K["gain_v"][:, :], K["gain_v"][:, :], 1.0 - LAMBDA_INIT, None, ALU.mult)
            dve.wait_ge(exped, 1)
            dve.tensor_tensor(K["neglam"][:, :], ex[:, 1:2], ex[:, 0:1], ALU.subtract).then_inc(seq, 1)
            dve.wait_ge(seq, 3)
            dve.tensor_scalar(K["neglam"][:, :], K["neglam"][:, :], -LAMBDA_INIT, None, ALU.add)

        @block.scalar
        def _(act):
            act.wait_ge(seq, 2)
            act.activation(ex[:, :], dot[:, :], ACT.Exp).then_inc(exped, 1)


def sample_attention(nc, D, K, S, H, NB, TS):
    HD = K["HD"]
    R = NB * TS
    HR = H * TS
    ROWS = 2 * HR
    NPG, PG = D["page_table"].shape[1], D["cache_k"].shape[1]
    assert PG == P
    PAST = NPG * PG
    KEYS = PAST + TS
    SCALE = float(HD) ** -0.5
    GP = 4
    NG = NPG // GP
    HH = H // 2
    with ExitStack() as ctx:
        m = Memory(nc, ctx, "smp")
        table = m.sb("table", [1, NB * NPG], I32)
        qrow, krow = m.sb("q_rows", [R, H * P]), m.sb("k_rows", [R, H * P])
        vnew = m.sb("v_new", [TS, H * P])
        qT, kn = m.sb("qT", [P, H, R]), m.sb("k_newT", [P, H, R])
        qd = m.sb("q_diag", [P, H * (ROWS + TS)])
        kp, vp = m.sb("k_page", [P, NPG, H * P]), m.sb("v_page", [P, NPG, H * P])
        kT = [m.sb(f"kT{i}", [P, H, GP * P]) for i in range(NG)]
        bias, pr = m.sb("bias", [ROWS, KEYS]), m.sb("probs", [ROWS, KEYS])
        low = m.sb("lowest", [ROWS, NG + 1])
        ssum, rsum, coef, lamc, tcol, scol = (m.sb(n, [ROWS, 1]) for n in ("sum", "rsum", "coef", "lamc", "t_col", "s_col"))
        sel, mc = m.sb("sel", [ROWS, HR]), m.sb("mix", [ROWS, HR])
        aT = m.sb("aT", [P, (NPG + 1) * HR])
        o = m.sb("o", [TS, H * P])
        ints = m.sb("ints", [ROWS, KEYS], I32)
        rowt, rows = m.sb("row_t", [ROWS, ROWS]), m.sb("row_s", [ROWS, ROWS])
        mask = m.sb("mask", [ROWS, TS])
        t_ps = [m.ps(f"t{i}", [P, HH, P]) for i in range(2)]
        s_ps = [m.ps(f"s{i}", [ROWS, GP * P]) for i in range(NG)]
        n_ps = m.ps("new", [ROWS, TS])
        a_ps = m.ps("a", [P, (NPG + 1) * HR])
        o_ps = m.ps("o_ps", [TS, H * P])
        row_in, tab_in, vn_in, o_out = (m.sem(n) for n in ("row_in", "tab_in", "vn_in", "o_out"))
        k_in = [m.sem(f"k_in{i}") for i in range(NPG)]
        v_in = [m.sem(f"v_in{i}") for i in range(NPG)]
        taken = [m.sem(f"taken{i}") for i in range(2)]
        (made, seq, r_turned, r_taken, q_ready, turned, scored, reduced, expd, mixed, a_turned, a_taken, applied,
         o_taken, passed) = (m.sem(n) for n in (
             "made", "seq", "r_turned", "r_taken", "q_ready", "turned", "scored", "reduced", "expd", "mixed",
             "a_turned", "a_taken", "applied", "o_taken", "passed"))
        block = m.block()
        tab_src = D["page_table"].rearrange("(o b) g -> o (b g)", o=1)

        def load_page(eng, tab, cache, b, g, dst, sem):
            n = eng.value_load(tab[0:1, ds(b * NPG + g, 1)], min_val=0, max_val=cache.shape[0] - 1)
            eng.dma_start(dst[:, g, :], cache[ds(n, 1), :, :, :].rearrange("o p h d -> (o p) (h d)")).then_inc(sem[g], 16)

        @block.sync
        def _(sp):
            def store(b):
                sp.wait_ge(o_taken, FREE + b + 1)
                sp.dma_start(D["o_rows"][ds(S + b * TS, TS), :], o[:, :]).then_inc(o_out, 16)

            sp.dma_start(table[:, :], tab_src).then_inc(tab_in, 16)
            sp.dma_start(qrow[:, :], D["q_rows"][S:S + R, :]).then_inc(row_in, 16)
            sp.dma_start(krow[:, :], D["k_sample"]).then_inc(row_in, 16)
            sp.wait_ge(tab_in, 16)

            def load_k(b, first=False):
                for g in range(NPG):
                    if not first:
                        sp.wait_ge(turned, (b - 1) * 2 * NPG + 2 * g + 2)
                    load_page(sp, table, D["cache_k"], b, g, kp, k_in)

            def load_v(b, first=False):
                if not first:
                    sp.wait_ge(applied, b)
                for g in range(NPG):
                    load_page(sp, table, D["cache_v"], b, g, vp, v_in)
                sp.dma_start(vnew[:, :], D["v_sample"][ds(b * TS, TS), :]).then_inc(vn_in, 16)

            load_k(0, True)
            load_k(1)
            load_v(0, True)
            with sp.Fori(2, NB) as b:
                load_k(b)
                load_v(b - 1)
                store(b - 2)
            load_v(NB - 1)
            store(NB - 2)
            store(NB - 1)
            sp.wait_ge(o_out, 16 + 16 * NB)

        @block.gpsimd
        def _(pool):
            pool.memset(qd[:, :], 0.0).then_inc(made, 1)
            rv = rows[:, :].rearrange("r (c h t) -> r c h t", c=2, h=H)
            for h in range(H):
                x = pool.memset(rv[:, :, h, :], 2.0 ** (-8.0 * (h + 1) / H) / SCALE)
            x.then_inc(made, 1)
            ti = ints[:, 0:ROWS].rearrange("r (c t) -> r c t", t=TS)
            pool.iota(ti, [[0, 2 * H], [1, TS]], base=0, channel_multiplier=0).then_inc(made, 1)
            pool.wait_ge(made, 3)
            pool.tensor_copy(rowt[:, :], ints[:, 0:ROWS]).then_inc(made, 1)
            pool.wait_ge(made, 4)
            pool.iota(ints[:, :], [[1, KEYS]], base=-PAST, channel_multiplier=0).then_inc(made, 1)
            pool.wait_ge(made, 5)
            pool.tensor_copy(bias[:, :], ints[:, :]).then_inc(made, 1)

        @block.vector
        def _(dve):
            c = Chain(dve, seq, 0)
            ident = K["ident"]
            dve.sem_inc(taken[1], FREE)
            dve.sem_inc(reduced, FREE)
            dve.wait_ge(made, 6)
            for row, col in ((rowt, tcol), (rows, scol)):
                c.link(dve.tensor_tensor_reduce(row[:, :], row[:, :], ident[0:ROWS, 0:ROWS], 1.0, 0.0, ALU.mult, ALU.add,
                                                col[:, :]))
            c.link(dve.tensor_scalar(bias[:, :], bias[:, :], tcol[:, 0:1], scol[:, 0:1], ALU.subtract, ALU.mult))
            c.link(dve.tensor_scalar(mask[:, :], bias[:, PAST:KEYS], 0.0, BIG, ALU.is_gt, ALU.mult))
            c.link(dve.tensor_tensor(bias[:, PAST:KEYS], bias[:, PAST:KEYS], mask[:, :], ALU.add))
            c.link(dve.tensor_copy(sel[0:HR, :], ident[0:HR, 0:HR]))
            c.link(dve.tensor_copy(sel[HR:ROWS, :], ident[HR:ROWS, HR:ROWS]))
            c.link(dve.memset(lamc[:, :], 1.0))
            c.link(dve.tensor_copy(lamc[HR:ROWS, :], K["neglam"][HR:ROWS, :]))
            SEQ0 = c.n
            for j in range(4):
                dst = qT if j < 2 else kn
                dve.wait_ge(r_turned, j + 1)
                dve.tensor_copy(dst[:, (j % 2) * HH:(j % 2 + 1) * HH, :], t_ps[j % 2][:, :, 0:R]).then_inc(r_taken, 1)

            def pages(b, first):
                if first:
                    dve.wait_ge(r_taken, 4)
                else:
                    dve.wait_ge(scored, b * (NG + 1))
                for comp in range(2):
                    part = slice(comp * HD, (comp + 1) * HD)
                    diag = qd[part, :].rearrange("p (h x) -> p h x", h=H)[:, :, comp * HR:comp * HR + TS]
                    x = dve.tensor_copy(diag, qT[part, :, ds(b * TS, TS)])
                    x.then_inc(q_ready, 1)
                for g in range(NPG):
                    dve.wait_ge(turned, b * 2 * NPG + 2 * g + 2)
                    dve.tensor_copy(kT[g // GP][:, HH:H, (g % GP) * P:(g % GP + 1) * P], t_ps[1][:, :, :]).then_inc(taken[1], 1)

            def take_a(b):
                dve.wait_ge(a_turned, b + 1)
                dve.tensor_copy(aT[:, 0:NPG * HR], a_ps[:, 0:NPG * HR])
                dve.tensor_copy(aT[0:TS, NPG * HR:], a_ps[0:TS, NPG * HR:]).then_inc(a_taken, 1)

            def reduce(b):
                for g in range(NG + 1):
                    ps = s_ps[g][:, :] if g < NG else n_ps[:, :]
                    cols = slice(g * GP * P, (g + 1) * GP * P) if g < NG else slice(PAST, KEYS)
                    if g:
                        dve.wait_ge(reduced, FREE + b * (NG + 1) + g)
                    dve.wait_ge(scored, b * (NG + 1) + g + 1)
                    dve.sem_inc(passed, 1)
                    dve.tensor_tensor_reduce(pr[:, cols], ps, bias[:, cols], -SCALE, low[:, g - 1:g] if g else -BIG,
                                             ALU.add, ALU.min, low[:, g:g + 1]).then_inc(reduced, 1)

            def weigh(b):
                dve.wait_ge(expd, b + 1)
                k = SEQ0 + 2 * b
                dve.reciprocal(rsum[:, :], ssum[:, :]).then_inc(seq, 1)
                dve.wait_ge(seq, k + 1)
                dve.tensor_tensor(coef[:, :], rsum[:, :], lamc[:, :], ALU.mult).then_inc(seq, 1)
                dve.wait_ge(seq, k + 2)
                dve.tensor_scalar(mc[:, :], sel[:, :], coef[:, 0:1], None, ALU.mult).then_inc(mixed, 1)

            pages(0, True)
            reduce(0)
            weigh(0)
            with dve.Fori(1, NB) as b:
                pages(b, False)
                take_a(b - 1)
                reduce(b)
                weigh(b)
            take_a(NB - 1)

        @block.scalar
        def _(act):
            act.sem_inc(taken[0], FREE)
            act.sem_inc(o_out, 16)

            def pages(b, first):
                for g in range(NPG):
                    act.wait_ge(turned, b * 2 * NPG + 2 * g + 1)
                    if g % GP == 0 and not first:
                        act.wait_ge(scored, (b - 1) * (NG + 1) + g // GP + 1)
                    act.activation(kT[g // GP][:, 0:HH, (g % GP) * P:(g % GP + 1) * P], t_ps[0][:, :, :], ACT.Copy
                                   ).then_inc(taken[0], 1)

            def exp(b):
                act.wait_ge(reduced, FREE + b * (NG + 1) + NG + 1)
                act.activation(pr[:, :], pr[:, :], ACT.Exp, scale=-1.0, bias=low[:, NG:NG + 1], accum_out=ssum[:, :]
                               ).then_inc(expd, 1)

            def result(b):
                act.wait_ge(applied, b + 1)
                act.wait_ge(o_out, 16 + 16 * b)
                act.activation(o[:, :], o_ps[:, :], ACT.Copy).then_inc(o_taken, 1)

            pages(0, True)
            exp(0)
            with act.Fori(1, NB) as b:
                pages(b, False)
                exp(b)
                result(b - 1)
            result(NB - 1)

        @block.tensor
        def _(pe):
            ident = K["ident"]
            pe.sem_inc(o_taken, FREE)
            pe.wait_ge(row_in, 32)
            for j in range(4):
                src = qrow if j < 2 else krow
                if j >= 2:
                    pe.wait_ge(r_taken, j - 1)
                for h in range(HH):
                    hh = (j % 2) * HH + h
                    x = pe.transpose(t_ps[j % 2][:, h, 0:R], src[:, hh * P:(hh + 1) * P], ident[0:R, 0:R])
                x.then_inc(r_turned, 1)
            pe.wait_ge(r_taken, 4)

            def q_of(h):
                return qd[:, h * ROWS:(h + 1) * ROWS]

            def score(b, first):
                for g in range(NPG):
                    pe.wait_ge(k_in[g], 16 * b + 16)
                    for j in range(2):
                        if not (first and g == 0):
                            pe.wait_ge(taken[j], FREE + b * NPG + g)
                        for h in range(HH):
                            hh = j * HH + h
                            x = pe.transpose(t_ps[j][:, h, :], kp[:, g, hh * P:(hh + 1) * P], ident[:, :])
                        x.then_inc(turned, 1)
                    if g % GP == GP - 1:
                        n = g // GP
                        for j in range(2):
                            pe.wait_ge(taken[j], FREE + b * NPG + g + 1)
                        if n == 0:
                            pe.wait_ge(q_ready, 2 * b + 2)
                        if not first:
                            pe.wait_ge(reduced, FREE + (b - 1) * (NG + 1) + n + 1)
                        for h in range(H):
                            x = pe.matmul(s_ps[n][:, :], q_of(h), kT[n][:, h, :], start=h == 0, stop=h == H - 1)
                        x.then_inc(scored, 1)
                if not first:
                    pe.wait_ge(reduced, FREE + b * (NG + 1))
                for h in range(H):
                    x = pe.matmul(n_ps[:, :], q_of(h), kn[:, h, ds(b * TS, TS)], start=h == 0, stop=h == H - 1)
                x.then_inc(scored, 1)

            def apply(b):
                pe.wait_ge(mixed, b + 1)
                for g in range(NPG + 1):
                    n = P if g < NPG else TS
                    x = pe.matmul(a_ps[0:n, g * HR:(g + 1) * HR], pr[:, g * P:g * P + n], mc[:, :], start=True, stop=True)
                x.then_inc(a_turned, 1)
                for g in range(NPG):
                    pe.wait_ge(v_in[g], 16 * b + 16)
                pe.wait_ge(vn_in, 16 * b + 16)
                pe.wait_ge(a_taken, b + 1)
                pe.wait_ge(o_taken, FREE + b)
                for h in range(H):
                    for g in range(NPG + 1):
                        n = P if g < NPG else TS
                        v = vp[:, g, h * P:(h + 1) * P] if g < NPG else vnew[:, h * P:(h + 1) * P]
                        x = pe.matmul(o_ps[:, h * P:(h + 1) * P], aT[0:n, g * HR + h * TS:g * HR + (h + 1) * TS], v,
                                      start=g == 0, stop=g == NPG)
                x.then_inc(applied, 1)

            score(0, True)
            with pe.Fori(1, NB) as b:
                score(b, False)
                apply(b - 1)
            apply(NB - 1)


def last_layer(nc, D, K, full, rest, H):
    w = D["w_out_b"][0]
    KC, N = w.shape[0] // P, w.shape[1]
    pairs = full // 2
    with ExitStack() as ctx:
        m = Memory(nc, ctx, "last")
        wst = [m.sb(f"wst{i}", [P, 2, N]) for i in range(2)]
        wh, wl = m.sb("w_hi", [P, KC, N], F32R), m.sb("w_lo", [P, KC, N], F32R)
        gf = m.sb("gain_f", [P, N])
        o, z, x1, sq, y = ([m.sb(f"{n}{i}", [P, N]) for i in range(2)] for n in ("o", "z", "x1", "sq", "y"))
        gh = [m.sb(f"g_hi{i}", [P, KC, P], F32R) for i in range(2)]
        gl = [m.sb(f"g_lo{i}", [P, KC, P], F32R) for i in range(2)]
        hs, hr, hq = ([m.sb(f"{n}{i}", [P, H]) for i in range(2)] for n in ("head_sum", "head_root", "head_r"))
        ys, yr, yq = ([m.sb(f"{n}{i}", [P, 1]) for i in range(2)] for n in ("row_sum", "row_root", "row_r"))
        t_ps = [m.ps(f"t{i}", [P, KC, P]) for i in range(2)]
        acc = [m.ps(f"acc{i}", [P, N]) for i in range(2)]
        w_sem, oz_sem, x_sem, out_sem = ([m.sem(f"{n}{i}") for i in range(2)] for n in ("w_in", "oz_in", "x1_in", "out"))
        (gf_in, whi, wlo, gated_z, squared, h_mean, h_root, seq, gated, turned, g_hi, g_lo, mm, added, y_sq, y_mean, y_root,
         recip, done) = (m.sem(n) for n in (
             "gf_in", "whi", "wlo", "gated_z", "squared", "h_mean", "h_root", "seq", "gated", "turned", "ghi", "glo", "mm",
             "added", "y_sq", "y_mean", "y_root", "recip", "done"))
        block = m.block()
        wv = w.rearrange("(k p) n -> p k n", p=P)

        def run(eng, pre, post):
            def pair(b, after=P):
                pre(b + 1, 1, P)
                post(b, 0, P)
                pre(b + 2, 0, after)
                post(b + 1, 1, P)

            pre(0, 0, P)
            pair(0)
            with eng.Fori(1, pairs - 1) as i:
                pair(2 * i)
            pair(full - 2, rest)
            post(full, 0, rest)

        @block.sync
        def _(sp):
            sp.dma_start(gf[:, :], D["norm_f_g"].partition_broadcast(P)).then_inc(gf_in, 16)

            def store(b, s, n):
                sp.wait_ge(done, b + 1)
                dst = D["y_rows"][ds(b * P, P), :] if n == P else D["ys_rows"]
                sp.dma_start(dst, y[s][0:n, :]).then_inc(out_sem[s], 16)

            def pre(b, s, n):
                if not (isinstance(b, int) and b < 2):
                    sp.wait_ge(turned, b - 1)
                for src, t in ((D["o_rows"], o), (D["z_rows"], z)):
                    sp.dma_start(t[s][0:n, :], src[ds(b * P, n), :]).then_inc(oz_sem[s], 16)
                if not (isinstance(b, int) and b < 2):
                    store(b - 2, s, P)
                sp.dma_start(x1[s][0:n, :], D["x1"][ds(b * P, n), :]).then_inc(x_sem[s], 16)

            for j in range(KC // 2):
                if j >= 2:
                    sp.wait_ge(wlo, 2 * (j - 1))
                sp.dma_start(wst[j % 2][:, :, :], wv[:, 2 * j:2 * j + 2, :]).then_inc(w_sem[j % 2], 16)
            pre(0, 0, P)
            pre(1, 1, P)
            with sp.Fori(1, pairs) as i:
                pre(2 * i, 0, P)
                pre(2 * i + 1, 1, P)
            pre(full, 0, rest)
            store(full - 1, 1, P)
            store(full, 0, rest)
            sp.wait_ge(out_sem[0], 16 * (pairs + 1))
            sp.wait_ge(out_sem[1], 16 * pairs)

        @block.gpsimd
        def _(pool):
            def gate(b, s, n):
                pool.wait_ge(oz_sem[s], 16 * (b - s) + 32)
                pool.tensor_tensor(z[s][0:n, :], o[s][0:n, :], z[s][0:n, :], ALU.mult).then_inc(gated_z, 1)

            run(pool, gate, lambda b, s, n: None)

        @block.scalar
        def _(act):
            for k in range(KC):
                act.wait_ge(w_sem[(k // 2) % 2], 16 * (k // 4) + 16)
                act.activation(wh[:, k, :], wst[(k // 2) % 2][:, k % 2, :], ACT.Copy, scale=K["gain_v"][:, 0:1]).then_inc(whi, 1)

            def pre(b, s, n):
                act.wait_ge(oz_sem[s], 16 * (b - s) + 32)
                if not (isinstance(b, int) and b < 2):
                    act.wait_ge(y_sq, b - 1)
                act.activation(sq[s][0:n, :], o[s][0:n, :], ACT.Square).then_inc(squared, 1)
                act.wait_ge(h_mean, b + 1)
                act.activation(hr[s][0:n, :], hs[s][0:n, :], ACT.Sqrt).then_inc(h_root, 1)
                act.wait_ge(turned, b + 1)
                if not (isinstance(b, int) and b < 2):
                    act.wait_ge(mm, b - 1)
                act.activation(gh[s][:, :, 0:n], t_ps[s][:, :, 0:n], ACT.Copy).then_inc(g_hi, 1)

            def post(b, s, n):
                act.wait_ge(added, b + 1)
                act.activation(sq[s][0:n, :], x1[s][0:n, :], ACT.Square, accum_out=ys[s][0:n, :]).then_inc(y_sq, 1)
                act.wait_ge(y_mean, b + 1)
                act.activation(yr[s][0:n, :], ys[s][0:n, :], ACT.Sqrt).then_inc(y_root, 1)

            run(act, pre, post)

        @block.vector
        def _(dve):
            for k in range(KC):
                dve.wait_ge(whi, k + 1)
                dve.scalar_tensor_tensor(out=wl[:, k, :], in0=wst[(k // 2) % 2][:, k % 2, :], scalar=K["gain_v"][:, 0:1],
                                         in1=f32(wh[:, k, :]), op0=ALU.mult, op1=ALU.subtract).then_inc(wlo, 1)
            dve.wait_ge(gf_in, 16)

            def pre(b, s, n):
                k = 2 * b
                heads = lambda t: t[0:n, :].rearrange("p (h v) -> p h v", h=H)
                dve.wait_ge(squared, b + 1)
                dve.tensor_reduce(hs[s][0:n, :], heads(sq[s]), AX_X, ALU.add).then_inc(seq, 1)
                dve.wait_ge(seq, k + 1)
                dve.tensor_scalar(hs[s][0:n, :], hs[s][0:n, :], float(H) / N, EPS, ALU.mult, ALU.add).then_inc(h_mean, 1)
                dve.wait_ge(h_root, b + 1)
                dve.reciprocal(hq[s][0:n, :], hr[s][0:n, :]).then_inc(seq, 1)
                dve.wait_ge(seq, k + 2)
                dve.wait_ge(gated_z, b + 1)
                dve.tensor_tensor(heads(o[s]), heads(z[s]), hq[s][0:n, :].unsqueeze(2).broadcast_to([n, H, N // H]),
                                  ALU.mult).then_inc(gated, 1)
                dve.wait_ge(g_hi, b + 1)
                dve.tensor_tensor(gl[s][:, :, 0:n], t_ps[s][:, :, 0:n], f32(gh[s][:, :, 0:n]), ALU.subtract).then_inc(g_lo, 1)

            def post(b, s, n):
                dve.wait_ge(mm, b + 1)
                dve.wait_ge(x_sem[s], 8 * (b - s) + 16)
                dve.tensor_tensor(x1[s][0:n, :], acc[s][0:n, :], x1[s][0:n, :], ALU.add).then_inc(added, 1)
                dve.wait_ge(y_sq, b + 1)
                dve.tensor_scalar(ys[s][0:n, :], ys[s][0:n, :], 1.0 / N, EPS, ALU.mult, ALU.add).then_inc(y_mean, 1)
                dve.wait_ge(y_root, b + 1)
                dve.reciprocal(yq[s][0:n, :], yr[s][0:n, :]).then_inc(recip, 1)
                dve.wait_ge(recip, b + 1)
                if not (isinstance(b, int) and b < 2):
                    dve.wait_ge(out_sem[s], 8 * (b - s))
                dve.scalar_tensor_tensor(out=y[s][0:n, :], in0=x1[s][0:n, :], scalar=yq[s][0:n, 0:1], in1=gf[0:n, :],
                                         op0=ALU.mult, op1=ALU.mult).then_inc(done, 1)

            run(dve, pre, post)

        @block.tensor
        def _(pe):
            ident = K["ident"]

            def pre(b, s, n):
                pe.wait_ge(gated, b + 1)
                if not (isinstance(b, int) and b < 2):
                    pe.wait_ge(g_lo, b - 1)
                for k in range(KC):
                    x = pe.transpose(t_ps[s][:, k, 0:n], o[s][0:n, k * P:(k + 1) * P], ident[0:n, 0:n])
                x.then_inc(turned, 1)

            def post(b, s, n):
                pe.wait_ge(g_lo, b + 1)
                if isinstance(b, int) and b == 0:
                    pe.wait_ge(wlo, KC)
                if not (isinstance(b, int) and b < 2):
                    pe.wait_ge(added, b - 1)
                for k in range(KC):
                    for c in range(N // 512):
                        cols = slice(c * 512, (c + 1) * 512)
                        last = three(pe, acc[s][0:n, cols], gh[s][:, k, 0:n], gl[s][:, k, 0:n],
                                     wh[:, k, cols], wl[:, k, cols], k == 0, k == KC - 1)
                last.then_inc(mm, 1)

            run(pe, pre, post)


def program(nc, D):
    S, DM = D["x_prompt"].shape[1:]
    NB, TS = D["x_sample"].shape[:2]
    R = NB * TS
    NT = S + R
    DA = D["w_in_a"].shape[2] // 2
    half = S // 2
    KC = DM // P
    D["gatedT"] = nc.dram_tensor("gatedT", (DA, NT), F32, kind="Internal").ap()
    for n in ("x1", "q_rows", "z_rows", "o_rows"):
        D[n] = nc.dram_tensor(n, (NT, DM), F32, kind="Internal").ap()
    for n in ("k_twice", "q_twice"):
        D[n] = nc.dram_tensor(n, (S, 2 * DM), F32, kind="Internal").ap()
    x_sample = D["x_sample"].rearrange("b t n -> (b t) n")
    for n in "kv":
        D[n + "_prompt"] = D[f"{n}_prompt_pages"].rearrange("b g p h d -> (b g p) (h d)")
        D[n + "_sample"] = D[f"{n}_sample_rows"].rearrange("b t h d -> (b t) (h d)")

    D["y_rows"] = D["y_prompt"].rearrange("b s n -> (b s) n")
    D["ys_rows"] = D["y_sample"].rearrange("b t n -> (b t) n")

    with ExitStack() as ctx:
        m = Memory(nc, ctx, "all")
        K = {"ident": m.sb("ident", [P, P])}
        with ExitStack() as front:
            f = Memory(nc, front, "front")
            K["win"] = f.sb("windows", [P, len(WINDOWS) * WROW])
            K["scale"] = f.sb("scale_a", [P, DA // P])
            K["carry"], K["carry2"] = f.sb("zeros", [P, DA // P, HIST]), f.sb("carry", [P, DA // P, HIST])
            K["stateT"] = f.sb("stateT", [P, DA // P, NB * HIST])
            K["tails"] = f.sb("tails", [P, DA // P, HIST + R])
            setup(nc, D, K)
            for h, T in enumerate((half, half + R)):
                with ExitStack() as part:
                    x = Memory(nc, part, f"a{h}")
                    xh, xl = x.sb("x_hi", [P, KC, T], F32R), x.sb("x_lo", [P, KC, T], F32R)
                    t0 = h * half
                    blocks = [(D["x_prompt"][0, t0 + b * P:t0 + (b + 1) * P, :], P) for b in range(half // P)]
                    if h:
                        blocks.append((x_sample, R))
                    prep(nc, f"prepa{h}", blocks, K["ident"], xh, xl, D["norm_a_g"][0], DM)
                    pool_layer(nc, h, D, K, xh, xl, T, half, t0, K["carry"] if h == 0 else K["carry2"],
                               K["carry2"])
            tails(nc, D, K, R)
        out_layer(nc, D, S // P, R, x_sample)
        with ExitStack() as part:
            g = Memory(nc, part, "g")
            gains = [g.sb(n, [P, KC]) for n in ("gain_kv", "gain_b")]
            load_columns(nc, "gains", [(gains[0], D["norm_kv_g"]), (gains[1], D["norm_b_g"][0])])
            for h, T in enumerate((half, half + R)):
                with ExitStack() as sub:
                    x = Memory(nc, sub, f"b{h}")
                    xh, xl = x.sb("x_hi", [P, KC, T], F32R), x.sb("x_lo", [P, KC, T], F32R)
                    t0 = h * half
                    blocks = [(D["x1"][t0 + b * P:t0 + min((b + 1) * P, T), :], min(P, T - b * P)) for b in range(-(-T // P))]
                    prep(nc, f"prepb{h}", blocks, K["ident"], xh, xl, None, DM)
                    project(nc, h, D, xh, xl, T, half, t0, gains)
        H = D["cache_k"].shape[2]
        K["neglam"], K["gain_v"] = m.sb("neg_lambda", [P, 1]), m.sb("gain_v", [P, 1])
        constants_b(nc, D, K)
        attention(nc, D, K, S, H)
        sample_attention(nc, D, K, S, H, NB, TS)
        last_layer(nc, D, K, S // P, R, H)


_INS = ["x_prompt", "x_sample", "cache_k", "cache_v", "state_pool", "page_table", "norm_a_g", "w_in_a", "w_map_a",
        "scale_a", "w_out_a", "norm_kv_g", "w_kv", "norm_b_g", "w_in_b", "lambda_q1", "lambda_k1", "lambda_q2",
        "lambda_k2", "subln_g", "w_out_b", "norm_f_g"]


def kernel(**inputs):
    import concourse.bacc as bacc
    from concourse.bass_utils import run_bass_kernel_spmd as run

    nc = bacc.Bacc("TRN2", target_bir_lowering=False, num_devices=1)
    arrays, D = {}, {}
    for name in _INS:
        a = np.ascontiguousarray(inputs[name])
        arrays[f"in_{name}"] = a
        D[name] = nc.dram_tensor(f"in_{name}", a.shape, mybir.dt.from_np(a.dtype), kind="ExternalInput").ap()
    (B, S, DM), (DB, TS, _) = inputs["x_prompt"].shape, inputs["x_sample"].shape
    _, page, H, KD = inputs["cache_k"].shape
    VD = inputs["cache_v"].shape[3]
    L, _, hist, DA = inputs["state_pool"].shape
    outs = {
        "y_prompt": (B, S, DM), "y_sample": (DB, TS, DM),
        "k_prompt_pages": (B, S // page, page, H, KD), "v_prompt_pages": (B, S // page, page, H, VD),
        "k_sample_rows": (DB, TS, H, KD), "v_sample_rows": (DB, TS, H, VD),
        "pool_prompt": (L, B, hist, DA), "pool_sample": (L, DB, hist, DA),
    }
    for name, shape in outs.items():
        D[name] = nc.dram_tensor(f"out_{name}", shape, F32, kind="ExternalOutput").ap()
    program(nc, D)
    r = run(nc, [arrays], core_ids=[0])
    return tuple(r.results[0][f"out_{name}"] for name in outs)
```

```python
import math
from contextlib import ExitStack

import numpy as np
import concourse.bass as bass
from concourse import mybir

ALU = mybir.AluOpType
ACT = mybir.ActivationFunctionType
F32 = mybir.dt.float32
F32R = mybir.dt.float32r
I32 = mybir.dt.int32
AX_X = mybir.AxisListType.X
ds = bass.ds

P = 128
EPS = 1e-6


class Chain:

    def __init__(self, engine, sem, base, steps=None):
        self.engine, self.sem, self.base, self.n, self.steps = engine, sem, base, 0, steps

    def done(self, instruction):
        self.n += 1
        instruction.then_inc(self.sem, 1)

    def wait(self):
        self.engine.wait_ge(self.sem, self.base + self.n)

    def link(self, instruction):
        self.done(instruction)
        self.wait()

    def close(self):
        assert self.steps is None or self.n == self.steps, (self.n, self.steps)


class Memory:

    def __init__(self, nc, ctx, part):
        self.nc, self.ctx, self.part, self.sems = nc, ctx, part, []

    def sb(self, name, shape, dt=F32):
        return self.ctx.enter_context(self.nc.sbuf_tensor(f"{self.part}_{name}", shape, dt))

    def ps(self, name, shape, dt=F32):
        return self.ctx.enter_context(self.nc.psum_tensor(f"{self.part}_{name}", shape, dt))

    def sem(self, name):
        s = self.ctx.enter_context(self.nc.semaphore(f"{self.part}_{name}"))
        self.sems.append(s)
        return s

    def block(self):
        self.ctx.callback(self.clear)
        return self.ctx.enter_context(self.nc.Block())

    def clear(self):
        with self.nc.Block() as block:
            @block.gpsimd
            def _(pool):
                for s in self.sems:
                    pool.sem_clear(s)


def f32(ap):
    return ap.bitcast(F32)


WINDOWS = (2, 4, 8, 16)
DOUBLINGS = (1, 2, 4, 8)
HIST = max(WINDOWS) - 1
FIRST = max(WINDOWS)
WROW = len(DOUBLINGS) + 1 + FIRST


LAYER_B = 1
LAMBDA_INIT = 0.8 - 0.6 * math.exp(-0.3 * LAYER_B)


def setup(nc, D, K):
    HD = D["lambda_q1"].shape[1]
    K["HD"] = HD
    NFB = K["stateT"].shape[1]
    rows = D["state_pool"].shape[1] * D["state_pool"].shape[2]
    with ExitStack() as ctx:
        m = Memory(nc, ctx, "setup")
        state = m.sb("state", [rows, NFB * P])
        pt = [m.ps(f"pt{i}", [P, 4, P]) for i in range(2)]
        vec = [m.sb(n, [P, HD]) for n in ("q1", "k1", "q2", "k2")]
        dot, ex, junk = m.sb("dot", [P, 2]), m.sb("ex", [P, 2]), m.sb("junk", [P, HD])
        state_in, made, turned, taken, columns_in, lam_in, seq, exped = (
            m.sem(n) for n in ("state_in", "made", "turned", "taken", "columns_in", "lam_in", "seq", "exped"))
        block = m.block()

        @block.sync
        def _(sp):
            sp.dma_start(state[:, :], D["state_pool"][0].rearrange("b t c -> (b t) c")).then_inc(state_in, 16)
            for t, n in zip(vec, ("lambda_q1", "lambda_k1", "lambda_q2", "lambda_k2")):
                sp.dma_start(t[:, :], D[n][0].partition_broadcast(P)).then_inc(lam_in, 16)
            columns = [(K["gain_v"], D["subln_g"][0]), (K["scale"], D["scale_a"][0]), (K["gain_kv"], D["norm_kv_g"]),
                       (K["gain_b"], D["norm_b_g"][0])]
            for tile, vector in columns:
                sp.dma_start(tile[:, :], vector.rearrange("(k p) -> p k", p=P),
                             allow_slow_non_contiguous=True).then_inc(columns_in, 16)
            sp.wait_ge(columns_in, 16 * len(columns))

        @block.gpsimd
        def _(pool):
            ident, win = K["ident"], K["win"]
            pool.memset(ident[:, :], 0.0).then_inc(made, 1)
            pool.wait_ge(made, 1)
            pool.affine_select(out=ident[:, :], in_=ident[:, :], compare_op=ALU.not_equal, fill=1.0, base=0,
                               pattern=[[-1, P]], channel_multiplier=1).then_inc(made, 1)
            pool.memset(K["carry"][:, :, :], 0.0)
            for g, w in enumerate(WINDOWS):
                o = g * WROW
                for i, s in enumerate(DOUBLINGS):
                    pool.memset(win[:, o + i:o + i + 1], 1.0 if s < w else 0.0)
                o += len(DOUBLINGS)
                pool.memset(win[:, o:o + 1], 1.0 / w)
                for t in range(w - 1):
                    pool.memset(win[:, o + 1 + t:o + 2 + t], 1.0 / (t + 1))
                pool.memset(win[:, o + w:o + 1 + FIRST], 1.0 / w)

        @block.tensor
        def _(pe):
            pe.wait_ge(made, 2)
            pe.wait_ge(state_in, 16)
            for q in range(NFB // 4):
                if q >= 2:
                    pe.wait_ge(taken, q - 1)
                for j in range(4):
                    t = pe.transpose(pt[q % 2][:, j, 0:rows], state[:, (4 * q + j) * P:(4 * q + j + 1) * P],
                                     K["ident"][0:rows, 0:rows])
                t.then_inc(turned, 1)

        @block.vector
        def _(dve):
            for q in range(NFB // 4):
                dve.wait_ge(turned, q + 1)
                dve.tensor_copy(K["stateT"][:, 4 * q:4 * q + 4, :], pt[q % 2][:, :, 0:rows]).then_inc(taken, 1)
            dve.wait_ge(lam_in, 64)
            for j in range(2):
                dve.tensor_tensor_reduce(junk[:, :], vec[2 * j][:, :], vec[2 * j + 1][:, :], 1.0, 0.0, ALU.mult, ALU.add,
                                         dot[:, j:j + 1]).then_inc(seq, 1)
                dve.wait_ge(seq, j + 1)
            dve.wait_ge(exped, 1)
            dve.tensor_tensor(K["neglam"][:, :], ex[:, 1:2], ex[:, 0:1], ALU.subtract).then_inc(seq, 1)
            dve.wait_ge(seq, 3)
            dve.tensor_scalar(K["neglam"][:, :], K["neglam"][:, :], -LAMBDA_INIT, None, ALU.add)
            dve.wait_ge(columns_in, 64)
            dve.tensor_scalar(K["gain_v"][:, :], K["gain_v"][:, :], 1.0 - LAMBDA_INIT, None, ALU.mult)

        @block.scalar
        def _(act):
            act.wait_ge(seq, 2)
            act.activation(ex[:, :], dot[:, :], ACT.Exp).then_inc(exped, 1)


def norm_stages(m, blocks, ident, xh, xl, slots, junk, small, banks, gain, width):

    NB, half, ring = len(blocks), width // P // 2, len(slots)
    ss, mean, root, rstd = (small[:, i * NB:(i + 1) * NB] for i in range(4))
    x_in = [m.sem(f"norm_x_in{i}") for i in range(ring)]
    gain_in, cleared, summed, averaged, rooted, inverted, scaled, turned, hi, lo = (m.sem("norm_" + n) for n in (
        "gain_in", "cleared", "summed", "averaged", "rooted", "inverted", "scaled", "turned", "hi", "lo"))

    def load(sp, b):
        src, n = blocks[b]
        if b >= ring:
            sp.wait_ge(turned, 2 * (b - ring + 1))
        sp.dma_start(slots[b % ring][0:n, :], src).then_inc(x_in[b % ring], 16)
        if b == 1 and gain:
            sp.dma_start(gain[0], gain[1].partition_broadcast(P)).then_inc(gain_in, 16)

    def measure(act, b):
        n = blocks[b][1]
        act.wait_ge(x_in[b % ring], 16 * (b // ring) + 16)
        act.wait_ge(cleared, 1)
        if b:
            act.wait_ge(summed, b)
        act.activation(junk[0:n, :], slots[b % ring][0:n, :], ACT.Square, accum_out=ss[0:n, b:b + 1]
                       ).then_inc(summed, 1)
        act.wait_ge(averaged, b + 1)
        act.activation(root[0:n, b:b + 1], mean[0:n, b:b + 1], ACT.Sqrt).then_inc(rooted, 1)

    def clear(dve):
        dve.memset(ss[:, :], 0.0).then_inc(cleared, 1)

    def scale(dve, b):
        n, x = blocks[b][1], slots[b % ring]
        dve.wait_ge(summed, b + 1)
        dve.wait_ge(cleared, 1)
        dve.tensor_scalar(mean[0:n, b:b + 1], ss[0:n, b:b + 1], 1.0 / width, EPS, ALU.mult, ALU.add
                          ).then_inc(averaged, 1)
        dve.wait_ge(rooted, b + 1)
        dve.reciprocal(rstd[0:n, b:b + 1], root[0:n, b:b + 1]).then_inc(inverted, 1)
        dve.wait_ge(inverted, b + 1)
        if gain is None:
            dve.tensor_scalar(x[0:n, :], x[0:n, :], rstd[0:n, b:b + 1], None, ALU.mult).then_inc(scaled, 1)
            return
        dve.wait_ge(gain_in, 16)
        dve.scalar_tensor_tensor(out=x[0:n, :], in0=x[0:n, :], scalar=rstd[0:n, b:b + 1], in1=gain[0][0:n, :],
                                 op0=ALU.mult, op1=ALU.mult).then_inc(scaled, 1)

    def turn(pe, b):
        n, x = blocks[b][1], slots[b % ring]
        pe.wait_ge(scaled, b + 1)
        for j in range(2):
            i = 2 * b + j
            if i >= len(banks):
                pe.wait_ge(lo, i + 1 - len(banks))
            for k in range(half):
                col = (j * half + k) * P
                t = pe.transpose(banks[i % len(banks)][:, k, 0:n], x[0:n, col:col + P], ident[0:n, 0:n])
            t.then_inc(turned, 1)

    def parts(b):
        n = blocks[b][1]
        for j in range(2):
            i = 2 * b + j
            yield i, banks[i % len(banks)][:, :, 0:n], (slice(None), slice(j * half, (j + 1) * half),
                                                                  slice(b * P, b * P + n))

    def high(act, b):
        for i, bank, at in parts(b):
            act.wait_ge(turned, i + 1)
            act.activation(xh[at], bank, ACT.Copy).then_inc(hi, 1)

    def low(dve, b):
        for i, bank, at in parts(b):
            dve.wait_ge(hi, i + 1)
            dve.tensor_tensor(xl[at], bank, f32(xh[at]), ALU.subtract).then_inc(lo, 1)

    return load, measure, clear, scale, turn, high, low, lo


def two_ahead(NB, ahead, behind, meanwhile, after=None):
    for b in range(2):
        ahead(b)
    meanwhile()
    for b in range(NB):
        if b + 2 < NB:
            ahead(b + 2)
        behind(b)
        if after:
            after(b)


FREE = 1


def three(pe, out, ah, al, bh, bl, first, last):
    pe.matmul(out, ah, bh, start=first, stop=False)
    pe.matmul(out, ah, bl, start=False, stop=False)
    return pe.matmul(out, al, bh, start=False, stop=last)


UNITS = [("u", 0), ("u", 1), ("u", 2), ("u", 3), ("z", 0), ("m", 0), ("z", 1), ("m", 1),
         ("z", 2), ("m", 2), ("z", 3), ("m", 3)]
NU = len(UNITS)
BY_ACT = [sum(k != "m" for k, _ in UNITS[:i + 1]) for i in range(NU)]
BY_DVE = [sum(k == "m" for k, _ in UNITS[:i + 1]) for i in range(NU)]


def pool_layer(nc, half, D, K, xh, xl, blocks, T, prompt, t0, carry_in, carry_out):
    KC = xh.shape[1]
    w_in, w_map = D["w_in_a"][0], D["w_map_a"][0]
    DA = w_in.shape[1] // 2
    NG = w_map.shape[0]
    GA = DA // NG
    GC = GA // P
    sample = T - prompt
    NB = D["state_pool"].shape[1]
    TS = sample // NB if sample else 0
    NCH = -(-T // 512)
    CW = T // NCH
    SEG = HIST + prompt + 1
    EW = SEG + (NB * (HIST + TS) if sample else 0)
    with ExitStack() as ctx:
        m = Memory(nc, ctx, f"pool{half}")
        wst = {"u": m.sb("wu", [P, KC, GA]), "z": m.sb("wz", [P, KC, GA]), "m": m.sb("wm", [P, GC, GA])}
        wh = [m.sb(f"wh{i}", [P, KC, P], F32R) for i in range(2)]
        wl = [m.sb(f"wl{i}", [P, KC, P], F32R) for i in range(2)]
        ext = [m.sb(f"ext{i}", [P, EW]) for i in range(2)]
        sa, sb_ = m.sb("sum_a", [P, EW]), m.sb("sum_b", [P, EW])
        mix = m.sb("mix", [P, T])
        mh, ml = m.sb("mix_hi", [P, GC, T], F32R), m.sb("mix_lo", [P, GC, T], F32R)
        cur = m.sb("cur", [P, WROW])
        first = m.sb("first", [P, FIRST])
        sz = [m.sb(f"silu_z{i}", [P, T]) for i in range(2)]
        gated = [m.sb(f"gated{i}", [P, T]) for i in range(2)]
        acc = [m.ps(f"acc{i}", [P, NCH, 512]) for i in range(2)]
        load_rows, measure, clear, scale, turn, high, low, halves_split = norm_stages(
            m, blocks, K["ident"], xh, xl, [t[:, 0:KC * P] for t in sz + gated], sa[:, 0:KC * P], mix,
                    [m.ps(f"turn{i}", [P, KC // 2, P]) for i in range(2)], (sb_[:, 0:KC * P], D["norm_a_g"][0]), KC * P)
        w_in_sem = {k: m.sem(f"w_{k}_in") for k in "uzm"}
        out_sem = [m.sem(f"gated_out{i}") for i in range(2)]
        zeroed, hi, lo, mm, taken_act, taken_dve, pooled, seq = (
            m.sem(n) for n in ("zeroed", "hi", "lo", "mm", "taken_act", "taken_dve", "pooled", "seq"))
        block = m.block()
        wv = w_in.rearrange("(k p) n -> p k n", p=P)
        nk = {"u": KC, "z": KC, "m": GC}

        def src(kind, g):
            if kind == "m":
                return w_map[ds(g, 1)].rearrange("o (k p) n -> p (o k) n", p=P)
            return wv[:, :, ds(g * GA + (DA if kind == "z" else 0), GA)]

        @block.sync
        def _(sp):
            def load(kind, g):
                sp.dma_start(wst[kind][:, :, :], src(kind, g)).then_inc(w_in_sem[kind], 16)

            def store(g, j):
                sp.wait_ge(taken_dve, FREE + g * GC + j + 1)
                sp.dma_start(D["gatedT"][ds(g * GA + j * P, P), t0:t0 + T], gated[j % 2][:, :]
                             ).then_inc(out_sem[j % 2], 16)

            def group(g, last):
                if not last:
                    sp.wait_ge(lo, g * NU + 4)
                    load("u", g + 1)
                for j in range(GC - 1):
                    store(g, j)
                if not last:
                    sp.wait_ge(lo, g * NU + NU)
                    load("z", g + 1)
                    load("m", g + 1)
                store(g, GC - 1)

            for s in out_sem:
                sp.sem_inc(s, 16)
            for b in range(2):
                load_rows(sp, b)
            load("u", 0)
            for b in range(2, len(blocks)):
                load_rows(sp, b)
            load("z", 0)
            load("m", 0)
            with sp.Fori(0, NG - 1) as g:
                group(g, False)
            group(NG - 1, True)
            for s in out_sem:
                sp.wait_ge(s, 16 + 16 * NG * GC // 2)

        @block.gpsimd
        def _(pool):
            for e in ext:
                pool.memset(e[:, :], 0.0).then_inc(zeroed, 1)

        @block.scalar
        def _(act):
            def split(g, i):
                kind, j = UNITS[i]
                act.wait_ge(w_in_sem[kind], 16 * g + 16)
                if not (isinstance(g, int) and g == 0 and i == 0):
                    act.wait_ge(mm, FREE + g * NU + i - 1)
                act.activation(wh[i % 2][:, 0:nk[kind], :], wst[kind][:, :, j * P:(j + 1) * P], ACT.Copy
                               ).then_inc(hi, 1)

            def take(g, i):
                kind, j = UNITS[i]
                if kind == "m":
                    return
                a = acc[i % 2]
                act.wait_ge(mm, FREE + g * NU + i + 1)
                if kind == "z":
                    act.wait_ge(taken_dve, FREE + g * GC + max(j - 1, 0))
                    act.activation(sz[j % 2][:, :].rearrange("p (c n) -> p c n", c=NCH), a[:, :, 0:CW], ACT.Silu
                                   ).then_inc(taken_act, 1)
                    return
                e = ext[j % 2]
                act.wait_ge(pooled, FREE + g * GC + max(j - 1, 0))
                fb = ds(g * GC + j, 1)
                act.activation(e[:, 0:HIST], carry_in[:, fb, :].rearrange("p o n -> p (o n)"), ACT.Copy)
                if not sample:
                    act.activation(carry_out[:, fb, :].rearrange("p o n -> p (o n)"), a[:, NCH - 1, CW - HIST:CW], ACT.Copy)
                    act.activation(e[:, HIST:HIST + T].rearrange("p (c n) -> p c n", c=NCH), a[:, :, 0:CW], ACT.Copy
                                   ).then_inc(taken_act, 1)
                    return
                full, rest = prompt // CW, prompt % CW
                act.activation(e[:, HIST:HIST + full * CW].rearrange("p (c n) -> p c n", c=full), a[:, 0:full, 0:CW],
                               ACT.Copy)
                act.activation(e[:, HIST + full * CW:HIST + prompt], a[:, full, 0:rest], ACT.Copy)
                new = a[:, full, rest:CW]
                seg = e[:, SEG:EW].rearrange("p (b t) -> p b t", b=NB)
                act.activation(seg[:, :, 0:HIST],
                               K["stateT"][:, fb, :].rearrange("p o (b t) -> p (o b) t", b=NB), ACT.Copy)
                act.activation(K["tails"][:, fb, 0:HIST].rearrange("p o n -> p (o n)"), a[:, full, rest - HIST:rest], ACT.Copy)
                act.activation(K["tails"][:, fb, HIST:HIST + sample].rearrange("p o n -> p (o n)"), new, ACT.Copy)
                act.activation(seg[:, :, HIST:HIST + TS], new.rearrange("p (b t) -> p b t", b=NB), ACT.Copy
                               ).then_inc(taken_act, 1)

            act.sem_inc(taken_act, FREE)
            act.wait_ge(zeroed, 2)
            two_ahead(len(blocks), lambda b: measure(act, b), lambda b: high(act, b), lambda: split(0, 0))

            def group(g, last):
                for i in range(NU):
                    if i + 1 < NU:
                        split(g, i + 1)
                    elif not last:
                        split(g + 1, 0)
                    take(g, i)

            with act.Fori(0, NG - 1) as g:
                group(g, False)
            group(NG - 1, True)

        STEPS = 1 + GC * (len(DOUBLINGS) + (3 if sample else 4))

        @block.vector
        def _(dve):
            def split(g, i):
                kind, j = UNITS[i]
                dve.wait_ge(hi, g * NU + i + 1)
                dve.tensor_tensor(wl[i % 2][:, 0:nk[kind], :], wst[kind][:, :, j * P:(j + 1) * P],
                                  f32(wh[i % 2][:, 0:nk[kind], :]), ALU.subtract).then_inc(lo, 1)

            def pool_unit(g, j, c):
                e = ext[j % 2]
                dve.wait_ge(taken_act, FREE + g * 2 * GC + BY_ACT[j])
                x, lead = e, 0
                for n, (s, y) in enumerate(zip(DOUBLINGS, (sa, sb_, sa, sb_))):
                    c.link(dve.scalar_tensor_tensor(out=y[:, lead + s:EW], in0=x[:, lead:EW - s],
                                                    scalar=cur[:, n:n + 1], in1=x[:, lead + s:EW],
                                                    op0=ALU.mult, op1=ALU.add))
                    x, lead = y, lead + s
                inv = cur[:, len(DOUBLINGS):len(DOUBLINGS) + 1]
                c.done(dve.scalar_tensor_tensor(out=mix[:, 0:prompt], in0=x[:, HIST:HIST + prompt], scalar=inv,
                                                in1=e[:, HIST:HIST + prompt], op0=ALU.mult, op1=ALU.subtract))
                if sample:
                    seg = slice(SEG, EW)
                    xs, es = (t[:, seg].rearrange("p (b t) -> p b t", b=NB)[:, :, HIST:HIST + TS] for t in (x, e))
                    c.link(dve.scalar_tensor_tensor(out=mix[:, prompt:T].rearrange("p (b t) -> p b t", b=NB), in0=xs,
                                                    scalar=inv, in1=es, op0=ALU.mult, op1=ALU.subtract))
                    c.link(dve.tensor_copy(mh[:, j, :], mix[:, :]))
                else:
                    c.link(dve.tensor_tensor(first[:, :], x[:, HIST:HIST + FIRST], cur[:, len(DOUBLINGS) + 1:WROW],
                                             ALU.mult))
                    c.link(dve.tensor_tensor(mix[:, 0:FIRST], first[:, :], e[:, HIST:HIST + FIRST], ALU.subtract))
                    c.link(dve.tensor_copy(mh[:, j, :], mix[:, :]))
                dve.tensor_tensor(ml[:, j, :], mix[:, :], f32(mh[:, j, :]), ALU.subtract).then_inc(pooled, 1)

            def gate(g, j):
                i = UNITS.index(("m", j))
                dve.wait_ge(mm, FREE + g * NU + i + 1)
                dve.wait_ge(taken_act, FREE + g * 2 * GC + BY_ACT[i])
                dve.wait_ge(out_sem[j % 2], 16 + g * (16 * GC // 2) + 16 * (j // 2))
                dve.scalar_tensor_tensor(out=gated[j % 2][:, :].rearrange("p (c n) -> p c n", c=NCH),
                                         in0=acc[i % 2][:, :, 0:CW], scalar=K["scale"][:, ds(g * GC + j, 1)],
                                         in1=sz[j % 2][:, :].rearrange("p (c n) -> p c n", c=NCH),
                                         op0=ALU.mult, op1=ALU.mult).then_inc(taken_dve, 1)

            def group(g, last):
                c = Chain(dve, seq, g * STEPS, STEPS)
                dve.wait_ge(pooled, FREE + g * GC)
                c.link(dve.tensor_copy(cur[:, :], K["win"][:, ds(g * WROW, WROW)]))
                for i, (kind, j) in enumerate(UNITS):
                    if i + 1 < NU:
                        split(g, i + 1)
                    elif not last:
                        split(g + 1, 0)
                    if kind == "u":
                        pool_unit(g, j, c)
                    elif kind == "m":
                        gate(g, j)
                c.close()

            dve.sem_inc(pooled, FREE)
            dve.sem_inc(taken_dve, FREE)
            clear(dve)
            two_ahead(len(blocks), lambda b: scale(dve, b), lambda b: low(dve, b), lambda: split(0, 0))
            with dve.Fori(0, NG - 1) as g:
                group(g, False)
            group(NG - 1, True)

        @block.tensor
        def _(pe):
            pe.sem_inc(mm, FREE)
            for b in range(len(blocks)):
                turn(pe, b)
            pe.wait_ge(halves_split, 2 * len(blocks))
            with pe.Fori(0, NG) as g:
                for i, (kind, j) in enumerate(UNITS):
                    pe.wait_ge(lo, g * NU + i + 1)
                    if kind == "m" and j == 0:
                        pe.wait_ge(pooled, FREE + g * GC + GC)
                    before = (i - 2) % NU
                    if UNITS[before][0] == "m":
                        pe.wait_ge(taken_dve, FREE + g * GC + (BY_DVE[before] if i >= 2 else 0))
                    else:
                        pe.wait_ge(taken_act, FREE + g * 2 * GC + (BY_ACT[before] if i >= 2 else 0))
                    mh_, ml_ = (mh, ml) if kind == "m" else (xh, xl)
                    for k in range(nk[kind]):
                        for c in range(NCH):
                            tok = slice(c * CW, (c + 1) * CW)
                            last = three(pe, acc[i % 2][:, c, 0:CW], wh[i % 2][:, k, :], wl[i % 2][:, k, :],
                                         mh_[:, k, tok], ml_[:, k, tok], k == 0, k == nk[kind] - 1)
                    last.then_inc(mm, 1)


def tails(nc, D, K, new):
    NFB = K["tails"].shape[1]
    rows = HIST + new
    NB, TS = D["pool_sample"].shape[1], new // D["pool_sample"].shape[1]
    with ExitStack() as ctx:
        m = Memory(nc, ctx, "tails")
        t = m.sb("rows", [rows, NFB * P])
        pt = [m.ps(f"pt{i}", [P, 4, P]) for i in range(2)]
        turned, taken, out = m.sem("turned"), m.sem("taken"), m.sem("out")
        block = m.block()

        @block.tensor
        def _(pe):
            for q in range(NFB // 4):
                if q >= 2:
                    pe.wait_ge(taken, q - 1)
                for j in range(4):
                    x = pe.transpose(pt[q % 2][0:rows, j, :], K["tails"][:, 4 * q + j, :], K["ident"][:, :])
                x.then_inc(turned, 1)

        @block.vector
        def _(dve):
            for q in range(NFB // 4):
                dve.wait_ge(turned, q + 1)
                dve.tensor_copy(t[:, 4 * q * P:4 * (q + 1) * P].rearrange("r (j n) -> r j n", j=4),
                                pt[q % 2][0:rows, :, :]).then_inc(taken, 1)

        @block.sync
        def _(sp):
            n = 1
            sp.dma_start(D["pool_sample"][0, :, 0:HIST - TS, :], D["state_pool"][0, :, TS:HIST, :]).then_inc(out, 16)
            sp.wait_ge(taken, NFB // 4)
            sp.dma_start(D["pool_prompt"][0, 0], t[0:HIST, :]).then_inc(out, 16)
            for b in range(NB):
                sp.dma_start(D["pool_sample"][0, b, HIST - TS:HIST, :], t[HIST + TS * b:HIST + TS * (b + 1), :]).then_inc(out, 16)
            sp.wait_ge(out, 16 * (2 + NB))


def out_layer(nc, D, full, rest, rows_x):
    w = D["w_out_a"][0]
    KC, N = w.shape[0] // P, w.shape[1]
    LK = 2
    with ExitStack() as ctx:
        m = Memory(nc, ctx, "outa")
        wst = [m.sb(f"wst{i}", [P, LK, N]) for i in range(2)]
        wh, wl = m.sb("w_hi", [P, KC, N], F32R), m.sb("w_lo", [P, KC, N], F32R)
        gst = [m.sb(f"gst{i}", [P, KC, P]) for i in range(2)]
        gh = [m.sb(f"g_hi{i}", [P, KC, P], F32R) for i in range(2)]
        gl = [m.sb(f"g_lo{i}", [P, KC, P], F32R) for i in range(2)]
        xs = [m.sb(f"x{i}", [P, N]) for i in range(2)]
        acc = [m.ps(f"acc{i}", [P, N]) for i in range(2)]
        w_sem, g_sem, x_sem, out_sem = ([m.sem(f"{n}{i}") for i in range(2)] for n in ("w_in", "g_in", "x_in", "out"))
        w_hi, w_lo, g_hi, g_lo, mm, added = (m.sem(n) for n in ("whi", "wlo", "ghi", "glo", "mm", "added"))
        block = m.block()
        wv = w.rearrange("(k p) n -> p k n", p=P)
        gv = D["gatedT"].rearrange("(k p) t -> p k t", p=P)
        pairs = full // 2

        @block.sync
        def _(sp):
            def load_g(b, s, n):
                sp.dma_start(gst[s][:, :, 0:n], gv[:, :, ds(b * P, n)]).then_inc(g_sem[s], 16)

            def load_x(b, s, n):
                src = D["x_prompt"][0, ds(b * P, n), :] if n == P else rows_x
                sp.dma_start(xs[s][0:n, :], src).then_inc(x_sem[s], 16)

            load_g(0, 0, P)
            load_g(1, 1, P)
            for i in range(KC // LK):
                if i >= 2:
                    sp.wait_ge(w_lo, i - 1)
                sp.dma_start(wst[i % 2][:, :, :], wv[:, i * LK:(i + 1) * LK, :]).then_inc(w_sem[i % 2], 16)
            load_x(0, 0, P)
            load_x(1, 1, P)

            def step(i, s, n):
                sp.wait_ge(added, 2 * i + s + 1)
                dst = D["x1"][ds((2 * i + s) * P, P), :]
                sp.dma_start(dst, xs[s][:, :]).then_inc(out_sem[s], 16)
                if n:
                    sp.wait_ge(g_lo, 2 * i + s + 1)
                    load_g(2 * i + s + 2, s, n)
                    sp.wait_ge(out_sem[s], 16 * i + 16)
                    load_x(2 * i + s + 2, s, n)

            with sp.Fori(0, pairs - 1) as i:
                step(i, 0, P)
                step(i, 1, P)
            step(pairs - 1, 0, rest)
            step(pairs - 1, 1, 0)
            sp.wait_ge(added, full + 1)
            sp.dma_start(D["x1"][full * P:full * P + rest, :], xs[0][0:rest, :]).then_inc(out_sem[0], 16)
            sp.wait_ge(out_sem[0], 16 * (pairs + 1))
            sp.wait_ge(out_sem[1], 16 * pairs)

        @block.scalar
        def _(act):
            def split(i, s, n):
                act.wait_ge(g_sem[s], 16 * i + 16)
                if not (isinstance(i, int) and i == 0):
                    act.wait_ge(mm, 2 * i + s - 1)
                act.activation(gh[s][:, :, 0:n], gst[s][:, :, 0:n], ACT.Copy).then_inc(g_hi, 1)

            split(0, 0, P)
            split(0, 1, P)
            for i in range(KC // LK):
                act.wait_ge(w_sem[i % 2], 16 * (i // 2) + 16)
                act.activation(wh[:, i * LK:(i + 1) * LK, :], wst[i % 2][:, :, :], ACT.Copy).then_inc(w_hi, 1)
            with act.Fori(1, pairs) as i:
                split(i, 0, P)
                split(i, 1, P)
            split(pairs, 0, rest)

        @block.vector
        def _(dve):
            def split(i, s, n):
                dve.wait_ge(g_hi, 2 * i + s + 1)
                dve.tensor_tensor(gl[s][:, :, 0:n], gst[s][:, :, 0:n], f32(gh[s][:, :, 0:n]), ALU.subtract).then_inc(g_lo, 1)

            def add(i, s, n):
                dve.wait_ge(mm, 2 * i + s + 1)
                dve.wait_ge(x_sem[s], 16 * i + 16)
                dve.tensor_tensor(xs[s][0:n, :], acc[s][0:n, :], xs[s][0:n, :], ALU.add).then_inc(added, 1)

            split(0, 0, P)
            split(0, 1, P)
            for i in range(KC // LK):
                dve.wait_ge(w_hi, i + 1)
                dve.tensor_tensor(wl[:, i * LK:(i + 1) * LK, :], wst[i % 2][:, :, :],
                                  f32(wh[:, i * LK:(i + 1) * LK, :]), ALU.subtract).then_inc(w_lo, 1)
            with dve.Fori(0, pairs - 1) as i:
                add(i, 0, P)
                split(i + 1, 0, P)
                add(i, 1, P)
                split(i + 1, 1, P)
            add(pairs - 1, 0, P)
            split(pairs, 0, rest)
            add(pairs - 1, 1, P)
            add(pairs, 0, rest)

        @block.tensor
        def _(pe):
            def product_k(s, n, k):
                for c in range(N // 512):
                    cols = slice(c * 512, (c + 1) * 512)
                    last = three(pe, acc[s][0:n, cols], gh[s][:, k, 0:n], gl[s][:, k, 0:n],
                                 wh[:, k, cols], wl[:, k, cols], k == 0, k == KC - 1)
                return last

            def product(i, s, n):
                pe.wait_ge(g_lo, 2 * i + s + 1)
                pe.wait_ge(added, 2 * i + s - 1)
                for k in range(KC):
                    last = product_k(s, n, k)
                last.then_inc(mm, 1)

            pe.wait_ge(g_lo, 2)
            for k in range(KC):
                pe.wait_ge(w_lo, k // LK + 1)
                for s in range(2):
                    last = product_k(s, P, k)
                    if k == KC - 1:
                        last.then_inc(mm, 1)
            with pe.Fori(1, pairs) as i:
                product(i, 0, P)
                product(i, 1, P)
            product(pairs, 0, rest)


def project(nc, half, D, K, xh, xl, blocks, T, prompt, t0, gains):
    KC = xh.shape[1]
    full, rest = prompt // P, T - prompt
    NB = full + (1 if rest else 0)
    CN = 512
    kinds = [("k", D["w_kv"], 0, 0), ("v", D["w_kv"], 1, 0), ("q", D["w_in_b"][0], 0, 1), ("z", D["w_in_b"][0], 1, 1)]
    W = D["w_kv"].shape[1] // 2
    NI = W // CN
    units = [(i, kd) for i in range(NI) for kd in kinds]
    with ExitStack() as ctx:
        m = Memory(nc, ctx, f"proj{half}")
        wst = [m.sb(f"wst{i}", [P, KC, CN]) for i in range(2)]
        wh = [m.sb(f"w_hi{i}", [P, KC, CN], F32R) for i in range(2)]
        wl = [m.sb(f"w_lo{i}", [P, KC, CN], F32R) for i in range(2)]
        NS = 5
        res = [m.sb(f"res{i}", [P, CN]) for i in range(NS)]
        acc = [m.ps(f"acc{i}", [P, CN]) for i in range(NS)]
        w_sem = [m.sem(f"w_in{i}") for i in range(2)]
        taken = [m.sem(f"taken{i}") for i in range(NS)]
        out_sem = [m.sem(f"out{i}") for i in range(NS)]
        hi, lo, mm = m.sem("hi"), m.sem("lo"), m.sem("mm")
        block = m.block()
        slot = [(b % 4, b // 4, P) if b < full else (4, 0, rest) for b in range(NB)]
        per = [full // 4] * 4 + [1]
        HD = D["lambda_q1"].shape[1]
        dup = [m.sb(f"twice{i}", [P, 2 * CN]) for i in range(2)]
        dup_out = [m.sem(f"twice_out{i}") for i in range(2)]
        doubled = m.sem("doubled")
        load_rows, measure, clear, scale, turn, high, low, halves_split = norm_stages(
            m, blocks, K["ident"], xh, xl, [m.sb(f"x{i}", [P, KC * P]) for i in range(3)], m.sb("junk", [P, KC * P]), m.sb("stats", [P, 4 * NB]),
                    [m.ps(f"turn{i}", [P, KC // 2, P]) for i in range(3)], None, KC * P)
        AHEAD = 3
        plan, stores, dups, last_dup = {}, [0] * NS, 0, [0] * NS
        for u, (i, kd) in enumerate(units):
            for b in range(NB):
                sl = slot[b][0]
                is_dup = kd[0] in "kq" and b < full
                is_store = not (kd[0] == "q" and b < full)
                plan[u, b] = (stores[sl], last_dup[sl], dups if is_dup else None, is_store)
                stores[sl] += is_store
                dups += is_dup
                if is_dup:
                    last_dup[sl] = dups

        def dest(kd, i, b):
            name, cols = kd[0], slice(i * CN, (i + 1) * CN)
            if name in "kv":
                return (D[name + "_prompt"][t0 + b * P:t0 + (b + 1) * P, cols] if b < full else D[name + "_sample"][:, cols])
            return D[name + "_rows"][t0 + b * P:t0 + b * P + slot[b][2], cols]

        @block.sync
        def _(sp):
            def load(u):
                i, kd = units[u]
                src = kd[1].rearrange("(k p) n -> p k n", p=P)[:, :, kd[2] * W + i * CN:kd[2] * W + (i + 1) * CN]
                sp.dma_start(wst[u % 2][:, :, :], src).then_inc(w_sem[u % 2], 16)

            for b in range(2):
                load_rows(sp, b)
            load(0)
            for b in range(2, NB):
                load_rows(sp, b)
            for u, (i, kd) in enumerate(units):
                if u + 1 < len(units):
                    if u >= 1:
                        sp.wait_ge(lo, u * KC)
                    load(u + 1)
                for b in range(NB):
                    s, nth, n = slot[b]
                    _, _, d, stored = plan[u, b]
                    if stored:
                        sp.wait_ge(taken[s], FREE + u * per[s] + nth + 1)
                        sp.dma_start(dest(kd, i, b), res[s][0:n, :]).then_inc(out_sem[s], 16)
                    if d is not None:
                        sp.wait_ge(doubled, d + 1)
                        rows = slice(t0 + b * P, t0 + (b + 1) * P)
                        sp.dma_start(D[kd[0] + "_twice"][rows, 2 * i * CN:2 * (i + 1) * CN], dup[d % 2][:, :]
                                     ).then_inc(dup_out[d % 2], 16)
            for s in range(NS if rest else NS - 1):
                sp.wait_ge(out_sem[s], 16 * stores[s])
            for s in range(2):
                sp.wait_ge(dup_out[s], 16 * dups // 2)

        @block.gpsimd
        def _(pool):
            for u, (i, kd) in enumerate(units):
                for b in range(NB):
                    s, nth, n = slot[b]
                    d = plan[u, b][2]
                    if d is None:
                        continue
                    pool.wait_ge(taken[s], FREE + u * per[s] + nth + 1)
                    if d >= 2:
                        pool.wait_ge(dup_out[d % 2], 16 * (d // 2))
                    pool.tensor_copy(dup[d % 2][:, :].rearrange("p (g j n) -> p g j n", j=2, n=HD),
                                     res[s][:, :].rearrange("p (g n) -> p g n", n=HD).unsqueeze(2)
                                     .broadcast_to([P, CN // HD, 2, HD])).then_inc(doubled, 1)

        def take(eng, u, b):
            s, nth, n = slot[b]
            eng.wait_ge(mm, u * NB + b + 1)
            stored, last, _, _ = plan[u, b]
            if stored:
                eng.wait_ge(out_sem[s], 16 * stored)
            if last:
                eng.wait_ge(doubled, last)
            return s, n

        @block.scalar
        def _(act):
            def split(u):
                gain = gains[units[u][1][3]]
                act.wait_ge(w_sem[u % 2], 16 * (u // 2) + 16)
                if u >= 2:
                    act.wait_ge(mm, (u - 1) * NB)
                for k in range(KC):
                    act.activation(wh[u % 2][:, k, :], wst[u % 2][:, k, :], ACT.Copy, scale=gain[:, k:k + 1]).then_inc(hi, 1)

            two_ahead(len(blocks), lambda b: measure(act, b), lambda b: high(act, b), lambda: split(0))
            for u, (i, kd) in enumerate(units):
                if u + 1 < len(units):
                    split(u + 1)
                if kd[0] == "z":
                    for b in range(NB):
                        s, n = take(act, u, b)
                        act.activation(res[s][0:n, :], acc[s][0:n, :], ACT.Silu).then_inc(taken[s], 1)

        @block.vector
        def _(dve):
            def split(u):
                gain = gains[units[u][1][3]]
                for k in range(KC):
                    dve.wait_ge(hi, u * KC + k + 1)
                    dve.scalar_tensor_tensor(out=wl[u % 2][:, k, :], in0=wst[u % 2][:, k, :], scalar=gain[:, k:k + 1],
                                             in1=f32(wh[u % 2][:, k, :]), op0=ALU.mult, op1=ALU.subtract).then_inc(lo, 1)

            def copy_out(u, b):
                s, n = take(dve, u, b)
                dve.tensor_copy(res[s][0:n, :], acc[s][0:n, :]).then_inc(taken[s], 1)

            def after(b):
                if b >= AHEAD:
                    copy_out(0, b - AHEAD)

            clear(dve)
            two_ahead(len(blocks), lambda b: scale(dve, b), lambda b: low(dve, b), lambda: split(0), after)
            for u, (i, kd) in enumerate(units):
                if u + 1 < len(units):
                    split(u + 1)
                if kd[0] != "z":
                    for b in range(NB - AHEAD if u == 0 else 0, NB):
                        copy_out(u, b)

        @block.tensor
        def _(pe):
            for t in taken:
                pe.sem_inc(t, FREE)
            for b in range(AHEAD):
                turn(pe, b)

            def unit(u, slot_u, first=False):
                pe.wait_ge(lo, u * KC + KC)
                for b in range(NB):
                    s, nth, n = slot[b]
                    if first:
                        pe.wait_ge(halves_split, 2 * b + 2)
                    pe.wait_ge(taken[s], FREE + u * per[s] + nth)
                    for k in range(KC):
                        last = three(pe, acc[s][0:n, :], xh[:, k, b * P:b * P + n], xl[:, k, b * P:b * P + n],
                                     wh[slot_u][:, k, :], wl[slot_u][:, k, :], k == 0, k == KC - 1)
                    last.then_inc(mm, 1)
                    if first and b + AHEAD < NB:
                        turn(pe, b + AHEAD)

            unit(0, 0, True)
            unit(1, 1)
            with pe.Fori(1, len(units) // 2) as i:
                unit(2 * i, 0)
                unit(2 * i + 1, 1)


BIG = -1e30
QUAD = 4


def attention(nc, D, K, S, H, LAG=2):
    NB = S // P
    HD = K["HD"]
    VD = P
    SCALE = float(HD) ** -0.5
    CH = 1024
    NSC = LAG + 1
    chunks = [[(c, k0, min(CH, (qb + 1) * P - k0)) for c in range(2) for k0 in range(0, (qb + 1) * P, CH)]
              for qb in range(NB)]
    first_chunk = [sum(len(c) for c in chunks[:qb]) for qb in range(NB + 1)]
    groups = [-(-(qb + 1) // QUAD) for qb in range(NB)]
    first_group = [sum(groups[:qb]) for qb in range(NB + 1)]
    NCHK, NGRP = first_chunk[NB], first_group[NB]
    assert NCHK % 2 == 0 and NGRP % 4 == 0 and H % 2 == 0
    NQ = NB // QUAD
    with ExitStack() as ctx:
        m = Memory(nc, ctx, "attn")
        kst, qst = (m.sb(n, [P, 2 * QUAD, 2 * P]) for n in ("k_st", "q_st"))
        v = [m.sb(f"v{i}", [P, NB, VD]) for i in range(2)]
        hi = [m.sb(f"kq_hi{i}", [P, 4, S], F32R) for i in range(2)]
        kl = [m.sb(f"k_lo{i}", [P, 2, S], F32R) for i in range(2)]
        bias = [m.sb(f"bias{i}", [P, S]) for i in range(2)]
        sc = [m.sb(f"scores{i}", [P, 2, S]) for i in range(NSC)]
        at = [m.sb(f"aT{i}", [P, QUAD, P]) for i in range(4)]
        ost = [m.sb(f"o_st{i}", [P, QUAD, VD]) for i in range(2)]
        low = [m.sb(f"lowest{i}", [P, 4]) for i in range(NSC)]
        sums = [m.sb(f"sums{i}", [P, 2]) for i in range(NSC)]
        inv = [m.sb(f"inv{i}", [P, 2]) for i in range(NSC)]
        coef = [m.sb(f"coef{i}", [P, 1]) for i in range(NSC)]
        s_ps = [m.ps(f"s{i}", [P, CH]) for i in range(2)]
        t_ps = [m.ps(f"t{i}", [P, QUAD, P]) for i in range(2)]
        o_ps = m.ps("o", [P, VD])
        x_ps = m.ps("x", [P, 4, P])
        quad_in = [m.sem(f"kq_in{p}") for p in range(2)]
        v_sem = [m.sem(f"v_in{i}") for i in range(2)]
        out_sem = [m.sem(f"o_out{i}") for i in range(2)]
        (scored, reduced, expd, combined, turned, taken, applied, o_done, x_turned, x_hi, x_lo, seq, bias_ok) = (
            m.sem(n) for n in ("scored", "reduced", "expd", "combined", "turned", "taken", "applied", "o_done",
                               "x_turned", "x_hi", "x_lo", "seq", "bias_ok"))
        made, passed, pool_passed = m.sem("made"), m.sem("passed"), m.sem("pool_passed")
        block = m.block()
        vrows = D["v_prompt"]

        def x_bank(h, kb):
            if not (isinstance(h, int) and h == 0):
                return x_ps, 1
            return ([x_ps] + [s[:, 0:4 * P].rearrange("p (j n) -> p j n", j=4) for s in s_ps])[kb % 3], 3

        def rows(src, h, b0, nb):
            return src[b0 * P:(b0 + nb) * P, ds(h * P, P)].rearrange("(b p) n -> p b n", p=P)

        def pairs(eng, body):
            with eng.Fori(0, H // 2 - 1) as i:
                body(2 * i, False)
                body(2 * i + 1, False, 1)
            body(H - 2, False)
            body(H - 1, True, 1)

        @block.sync
        def _(sp):
            def load_kq(h, p):
                s = p % 2
                for src, dst in ((D["k_twice"], kst), (D["q_twice"], qst)):
                    sp.dma_start(dst[:, s * QUAD:(s + 1) * QUAD, :],
                                 src[p * QUAD * P:(p + 1) * QUAD * P, ds(h * 2 * P, 2 * P)]
                                 .rearrange("(b p) n -> p b n", p=P)).then_inc(quad_in[s], 16)

            def after(h, p):
                load_kq(h + (p + 2) // NQ, (p + 2) % NQ)

            def load_v(h, s):
                sp.dma_start(v[s][:, :, :], rows(vrows, h, 0, NB)).then_inc(v_sem[s], 16)

            for s in out_sem:
                sp.sem_inc(s, 16)
            load_kq(0, 0)
            load_kq(0, 1)
            load_v(0, 0)
            for p in range(NQ):
                sp.wait_ge(x_turned, p * QUAD + QUAD)
                after(0, p)

            def head(h, last, a=0):
                if not last:
                    sp.wait_ge(applied, QUAD + h * NGRP)
                    load_v(h + 1, 1 - a)
                for p in range(NQ):
                    if not isinstance(h, int) or h + 1 + (p + 2) // NQ < H:
                        sp.wait_ge(x_turned, (h + 1) * NB + (p + 1) * QUAD)
                        after(h + 1, p)
                    sp.wait_ge(o_done, FREE + h * NB + (p + 1) * QUAD)
                    dst = D["o_rows"][p * QUAD * P:(p + 1) * QUAD * P, ds(h * P, P)].rearrange("(b p) n -> p b n", p=P)
                    sp.dma_start(dst, ost[p % 2][:, :, :]).then_inc(out_sem[p % 2], 16)

            pairs(sp, head)
            for s in out_sem:
                sp.wait_ge(s, 16 + 16 * H * NQ // 2)

        @block.gpsimd
        def _(pool):
            dist = sc[1][:, 0, :].bitcast(I32)
            slope0 = 2.0 ** (-8.0 / H) / SCALE
            pool.iota(dist, [[1, S]], base=P - S, channel_multiplier=-1).then_inc(made, 1)
            pool.wait_ge(made, 1)
            pool.tensor_scalar(bias[0][:, :], dist, slope0, None, ALU.mult).then_inc(made, 1)
            pool.wait_ge(made, 2)
            pool.affine_select(out=bias[0][:, :], in_=bias[0][:, :], compare_op=ALU.is_ge, fill=BIG, base=S - P,
                               pattern=[[-1, S]], channel_multiplier=1).then_inc(bias_ok, 1)

            def head(h, last, a=0):
                if last:
                    return
                pool.wait_ge(bias_ok, h + 1)
                pool.wait_ge(reduced, 2 + h * NCHK)
                pool.sem_inc(pool_passed, 1)
                pool.tensor_scalar(bias[1 - a][:, :], bias[a][:, :], 2.0 ** (-8.0 / H), None, ALU.mult).then_inc(bias_ok, 1)

            pairs(pool, head)

        @block.tensor
        def _(pe):
            def turn_kq(h, kb, s):
                if kb % QUAD == 0:
                    p = kb // QUAD
                    pe.wait_ge(quad_in[p % 2], 32 * (h * (NQ // 2) + p // 2) + 32)
                bank, banks = x_bank(h, kb)
                if not (isinstance(h, int) and h == 0 and kb < banks):
                    pe.wait_ge(x_lo, h * NB + kb + 1 - banks)
                for j, src in enumerate((kst, qst)):
                    for c in range(2):
                        last = pe.transpose(bank[:, 2 * j + c, :], src[:, kb % (2 * QUAD), c * P:(c + 1) * P],
                                            K["ident"][:, :])
                last.then_inc(x_turned, 1)

            def score(h, a, qb, which):
                if qb == 0 and 0 in which:
                    pe.wait_ge(x_lo, h * NB + NB)
                for x in which:
                    c, k0, n = chunks[qb][x]
                    idx = first_chunk[qb] + x
                    out = s_ps[idx % 2]
                    pe.wait_ge(reduced, 2 + h * NCHK + idx - 1)
                    qc = hi[a][:, 2 + c, qb * P:(qb + 1) * P]
                    for o in range(0, n, 512):
                        w = min(512, n - o)
                        keys = slice(k0 + o, k0 + o + w)
                        pe.matmul(out[:, o:o + w], qc, hi[a][:, c, keys], start=True, stop=False)
                        last = pe.matmul(out[:, o:o + w], qc, kl[a][:, c, keys], start=False, stop=True)
                    last.then_inc(scored, 1)

            def turn(h, a, qb, g):
                idx = first_group[qb] + g
                if g == 0:
                    pe.wait_ge(combined, h * NB + qb + 1)
                pe.wait_ge(taken, 2 + h * NGRP + idx - 1)
                for kb in range(g * QUAD, min((g + 1) * QUAD, qb + 1)):
                    last = pe.transpose(t_ps[idx % 2][:, kb % QUAD, :], sc[(a * NB + qb) % NSC][:, 0, kb * P:(kb + 1) * P],
                                        K["ident"][:, :])
                last.then_inc(turned, 1)

            def apply(h, a, qb, g):
                idx = first_group[qb] + g
                pe.wait_ge(taken, 2 + h * NGRP + idx + 1)
                if g == 0:
                    pe.wait_ge(o_done, FREE + h * NB + qb)
                    if qb == 0:
                        pe.wait_ge(v_sem[a], 8 * (h - a) + 16)
                for kb in range(g * QUAD, min((g + 1) * QUAD, qb + 1)):
                    last = pe.matmul(o_ps[:, :], at[idx % 4][:, kb % QUAD, :], v[a][:, kb, :], start=kb == 0, stop=kb == qb)
                last.then_inc(applied, 1)

            def out_groups(h, a, qb, gs):
                gs = list(gs)
                for n, g in enumerate(gs):
                    if n == 0:
                        turn(h, a, qb, g)
                    if n + 1 < len(gs):
                        turn(h, a, qb, gs[n + 1])
                    apply(h, a, qb, g)

            pe.sem_inc(taken, 2)
            pe.sem_inc(reduced, 2)
            pe.sem_inc(o_done, FREE)
            for kb in range(NB):
                turn_kq(0, kb, 0)
            state = []

            def head(h, last, a=0):
                for qb in range(NB):
                    nx = len(chunks[qb])
                    score(h, a, qb, range(nx // 2))
                    back = state.pop(0) if len(state) >= LAG else None
                    if back:
                        ng = groups[back[2]]
                        out_groups(*back, range(0, (ng + 1) // 2))
                    if not last:
                        turn_kq(h + 1, qb, 1 - a)
                    score(h, a, qb, range(nx // 2, nx))
                    if back:
                        out_groups(*back, range((ng + 1) // 2, ng))
                    state.append((h, a, qb))
                if a == 1:
                    while state:
                        back = state.pop(0)
                        out_groups(*back, range(groups[back[2]]))

            pairs(pe, head)

        @block.scalar
        def _(act):
            act.sem_inc(applied, QUAD)

            def exp(h, a, qb, c):
                s = (a * NB + qb) % NSC
                n = (qb + 1) * P
                last = max(x for x, ch in enumerate(chunks[qb]) if ch[0] == c)
                act.wait_ge(reduced, 2 + h * NCHK + first_chunk[qb] + last + 1)
                col = 2 * ((n - 1) // CH) + c
                act.activation(sc[s][:, c, 0:n], sc[s][:, c, 0:n], ACT.Exp, scale=-1.0, bias=low[s][:, col:col + 1],
                               accum_out=sums[s][:, c:c + 1]).then_inc(expd, 1)

            def take(h, a, qb, gs):
                for g in gs:
                    idx = first_group[qb] + g
                    n = min(QUAD, qb + 1 - g * QUAD)
                    act.wait_ge(turned, h * NGRP + idx + 1)
                    act.wait_ge(applied, QUAD + h * NGRP + idx - 3)
                    act.activation(at[idx % 4][:, 0:n, :], t_ps[idx % 2][:, 0:n, :], ACT.Copy).then_inc(taken, 1)

            def result(h, a, qb):
                q = qb // QUAD
                act.wait_ge(applied, QUAD + h * NGRP + first_group[qb + 1])
                if qb % QUAD == 0:
                    act.wait_ge(out_sem[q % 2], 16 + h * (16 * NQ // 2) + 16 * (q // 2))
                act.activation(ost[q % 2][:, qb % QUAD, :], o_ps[:, :], ACT.Copy,
                               scale=inv[(a * NB + qb) % NSC][:, 0:1]).then_inc(o_done, 1)

            def turned_kq(h, kb, s):
                act.wait_ge(x_turned, h * NB + kb + 1)
                act.activation(hi[s][:, :, kb * P:(kb + 1) * P], x_bank(h, kb)[0][:, :, :], ACT.Copy).then_inc(x_hi, 1)

            for kb in range(NB):
                turned_kq(0, kb, 0)
            state = []

            def head(h, last, a=0):
                for qb in range(NB):
                    back = state.pop(0) if len(state) >= LAG else None
                    if back:
                        ng = groups[back[2]]
                        take(*back, range(0, (ng + 1) // 2))
                    exp(h, a, qb, 0)
                    if not last:
                        turned_kq(h + 1, qb, 1 - a)
                    if back:
                        take(*back, range((ng + 1) // 2, ng))
                    exp(h, a, qb, 1)
                    if back:
                        result(*back)
                    state.append((h, a, qb))
                if a == 1:
                    while state:
                        back = state.pop(0)
                        take(*back, range(groups[back[2]]))
                        result(*back)

            pairs(act, head)

        @block.vector
        def _(dve):
            def reduce(h, a, qb, which):
                s = (a * NB + qb) % NSC
                for x in which:
                    c, k0, n = chunks[qb][x]
                    idx = first_chunk[qb] + x
                    if x == 0 and not (a == 0 and qb < NSC):
                        b, q = divmod(a * NB + qb - NSC, NB)
                        dve.wait_ge(turned, (h - a + b) * NGRP + first_group[q + 1])
                    if qb == 0 and x == 0:
                        dve.wait_ge(bias_ok, h + 1)
                    ch = k0 // CH
                    if ch:
                        dve.wait_ge(reduced, 2 + h * NCHK + idx)
                    b0 = S - (qb + 1) * P + k0
                    dve.wait_ge(scored, h * NCHK + idx + 1)
                    dve.sem_inc(passed, 1)
                    dve.tensor_tensor_reduce(sc[s][:, c, k0:k0 + n], s_ps[idx % 2][:, 0:n], bias[a][:, b0:b0 + n], -SCALE,
                                             low[s][:, 2 * ch - 2 + c:2 * ch - 1 + c] if ch else -BIG, ALU.add, ALU.min,
                                             low[s][:, 2 * ch + c:2 * ch + c + 1]).then_inc(reduced, 1)

            def combine(h, a, qb):
                s = (a * NB + qb) % NSC
                n = (qb + 1) * P
                k = h * 2 * NB + 2 * qb
                dve.wait_ge(expd, h * 2 * NB + 2 * qb + 2)
                if not (a == 0 and qb < NSC):
                    b, q = divmod(a * NB + qb - NSC, NB)
                    dve.wait_ge(o_done, FREE + (h - a + b) * NB + q + 1)
                dve.reciprocal(inv[s][:, :], sums[s][:, :]).then_inc(seq, 1)
                dve.wait_ge(seq, k + 1)
                dve.scalar_tensor_tensor(out=coef[s][:, :], in0=sums[s][:, 0:1], scalar=inv[s][:, 1:2], in1=K["neglam"][:, :],
                                         op0=ALU.mult, op1=ALU.mult).then_inc(seq, 1)
                dve.wait_ge(seq, k + 2)
                dve.scalar_tensor_tensor(out=sc[s][:, 0, 0:n], in0=sc[s][:, 1, 0:n], scalar=coef[s][:, 0:1],
                                         in1=sc[s][:, 0, 0:n], op0=ALU.mult, op1=ALU.add).then_inc(combined, 1)

            def split_kq(h, kb, s):
                blk = slice(kb * P, (kb + 1) * P)
                dve.wait_ge(x_hi, h * NB + kb + 1)
                bank = x_bank(h, kb)[0]
                dve.tensor_tensor(kl[s][:, :, blk], bank[:, 0:2, :], f32(hi[s][:, 0:2, blk]), ALU.subtract)
                dve.tensor_tensor(hi[s][HD:P, 2:4, blk], bank[HD:P, 2:4, :], f32(hi[s][HD:P, 2:4, blk]),
                                  ALU.subtract).then_inc(x_lo, 1)

            for kb in range(NB):
                split_kq(0, kb, 0)
            state = []

            def head(h, last, a=0):
                for qb in range(NB):
                    nx = len(chunks[qb])
                    back = state.pop(0) if state else None
                    reduce(h, a, qb, range(nx // 2))
                    if back:
                        combine(*back)
                    reduce(h, a, qb, range(nx // 2, nx))
                    if not last:
                        split_kq(h + 1, qb, 1 - a)
                    state.append((h, a, qb))
                if a == 1:
                    while state:
                        combine(*state.pop(0))

            pairs(dve, head)


def sample_attention(nc, D, K, S, H, NB, TS):
    HD = K["HD"]
    R = NB * TS
    HR = H * TS
    ROWS = 2 * HR
    NPG, PG = D["page_table"].shape[1], D["cache_k"].shape[1]
    assert PG == P
    PAST = NPG * PG
    KEYS = PAST + TS
    SCALE = float(HD) ** -0.5
    GP = 4
    NG = NPG // GP
    HH = H // 2
    with ExitStack() as ctx:
        m = Memory(nc, ctx, "smp")
        table = m.sb("table", [1, NB * NPG], I32)
        qrow, krow = m.sb("q_rows", [R, H * P]), m.sb("k_rows", [R, H * P])
        vnew = m.sb("v_new", [TS, H * P])
        qT, kn = m.sb("qT", [P, H, R]), m.sb("k_newT", [P, H, R])
        qd = m.sb("q_diag", [P, H * (ROWS + TS)])
        kp, vp = m.sb("k_page", [P, NPG, H * P]), m.sb("v_page", [P, NPG, H * P])
        kT = [m.sb(f"kT{i}", [P, H, GP * P]) for i in range(NG)]
        bias, pr = m.sb("bias", [ROWS, KEYS]), m.sb("probs", [ROWS, KEYS])
        low = m.sb("lowest", [ROWS, NG + 1])
        ssum, rsum, coef, lamc, tcol, scol = (m.sb(n, [ROWS, 1]) for n in ("sum", "rsum", "coef", "lamc", "t_col", "s_col"))
        sel, mc = m.sb("sel", [ROWS, HR]), m.sb("mix", [ROWS, HR])
        aT = m.sb("aT", [P, (NPG + 1) * HR])
        o = m.sb("o", [HR, H * P])
        ints = m.sb("ints", [ROWS, KEYS], I32)
        rowt, rows = m.sb("row_t", [ROWS, ROWS]), m.sb("row_s", [ROWS, ROWS])
        mask = m.sb("mask", [ROWS, TS])
        t_ps = [[m.ps(f"t{i}{s}", [P, HH, P]) for s in range(2)] for i in range(2)]
        s_ps = [m.ps(f"s{i}", [ROWS, GP * P]) for i in range(NG)]
        an_ps = m.ps("a_new", [P, (NPG + 1) * HR + TS])
        a_ps, n_ps = an_ps[:, 0:(NPG + 1) * HR], an_ps[0:ROWS, (NPG + 1) * HR:]
        o_ps = m.ps("o_ps", [HR, HH * P])
        row_in, tab_in, vn_in, o_out = (m.sem(n) for n in ("row_in", "tab_in", "vn_in", "o_out"))
        k_in = [m.sem(f"k_in{i}") for i in range(NPG)]
        v_in = [m.sem(f"v_in{i}") for i in range(NPG)]
        taken = [m.sem(f"taken{i}") for i in range(2)]
        (made, seq, r_turned, r_taken, q_ready, turned, scored, reduced, expd, mixed, a_turned, a_taken, applied,
         o_taken, passed) = (m.sem(n) for n in (
             "made", "seq", "r_turned", "r_taken", "q_ready", "turned", "scored", "reduced", "expd", "mixed",
             "a_turned", "a_taken", "applied", "o_taken", "passed"))
        block = m.block()
        tab_src = D["page_table"].rearrange("(o b) g -> o (b g)", o=1)

        def load_page(eng, tab, cache, b, g, dst, sem):
            n = eng.value_load(tab[0:1, ds(b * NPG + g, 1)], min_val=0, max_val=cache.shape[0] - 1)
            eng.dma_start(dst[:, g, :], cache[ds(n, 1), :, :, :].rearrange("o p h d -> (o p) (h d)")).then_inc(sem[g], 16)

        @block.sync
        def _(sp):
            sp.dma_start(table[:, :], tab_src).then_inc(tab_in, 16)
            sp.dma_start(qrow[:, :], D["q_rows"][S:S + R, :]).then_inc(row_in, 16)
            sp.dma_start(krow[:, :], D["k_sample"]).then_inc(row_in, 16)
            sp.wait_ge(tab_in, 16)

            def load_k(b, first=False):
                for g in range(NPG):
                    if not first:
                        sp.wait_ge(turned, (b - 1) * 2 * NPG + 2 * g + 2)
                    load_page(sp, table, D["cache_k"], b, g, kp, k_in)

            def load_v(b, first=False):
                if not first:
                    sp.wait_ge(applied, 2 * b)
                for g in range(NPG):
                    load_page(sp, table, D["cache_v"], b, g, vp, v_in)
                sp.dma_start(vnew[:, :], D["v_sample"][ds(b * TS, TS), :]).then_inc(vn_in, 16)

            def store(b):
                sp.wait_ge(o_taken, FREE + 2 * b + 2)
                for h in range(H):
                    sp.dma_start(D["o_rows"][ds(S + b * TS, TS), h * P:(h + 1) * P], o[h * TS:(h + 1) * TS, h * P:(h + 1) * P]
                                 ).then_inc(o_out, 16)

            sp.sem_inc(o_out, 16)
            load_k(0, True)
            load_k(1)
            load_v(0, True)
            with sp.Fori(2, NB) as b:
                load_k(b)
                load_v(b - 1)
                store(b - 2)
            load_v(NB - 1)
            store(NB - 2)
            store(NB - 1)
            sp.wait_ge(o_out, 16 + 16 * H * NB)

        @block.gpsimd
        def _(pool):
            pool.memset(qd[:, :], 0.0).then_inc(made, 1)
            rv = rows[:, :].rearrange("r (c h t) -> r c h t", c=2, h=H)
            for h in range(H):
                x = pool.memset(rv[:, :, h, :], 2.0 ** (-8.0 * (h + 1) / H) / SCALE)
            x.then_inc(made, 1)
            ti = ints[:, 0:ROWS].rearrange("r (c t) -> r c t", t=TS)
            pool.iota(ti, [[0, 2 * H], [1, TS]], base=0, channel_multiplier=0).then_inc(made, 1)
            pool.wait_ge(made, 3)
            pool.tensor_copy(rowt[:, :], ints[:, 0:ROWS]).then_inc(made, 1)
            pool.wait_ge(made, 4)
            pool.iota(ints[:, :], [[1, KEYS]], base=-PAST, channel_multiplier=0).then_inc(made, 1)
            pool.wait_ge(made, 5)
            pool.tensor_copy(bias[:, :], ints[:, :]).then_inc(made, 1)

        @block.vector
        def _(dve):
            c = Chain(dve, seq, 0)
            ident = K["ident"]
            dve.sem_inc(taken[1], FREE)
            dve.sem_inc(reduced, FREE)
            dve.wait_ge(made, 6)
            for row, col in ((rowt, tcol), (rows, scol)):
                c.link(dve.tensor_tensor_reduce(row[:, :], row[:, :], ident[0:ROWS, 0:ROWS], 1.0, 0.0, ALU.mult, ALU.add,
                                                col[:, :]))
            c.link(dve.tensor_scalar(bias[:, :], bias[:, :], tcol[:, 0:1], scol[:, 0:1], ALU.subtract, ALU.mult))
            c.link(dve.tensor_scalar(mask[:, :], bias[:, PAST:KEYS], 0.0, BIG, ALU.is_gt, ALU.mult))
            c.link(dve.tensor_tensor(bias[:, PAST:KEYS], bias[:, PAST:KEYS], mask[:, :], ALU.add))
            c.link(dve.tensor_copy(sel[0:HR, :], ident[0:HR, 0:HR]))
            c.link(dve.tensor_copy(sel[HR:ROWS, :], ident[HR:ROWS, HR:ROWS]))
            c.link(dve.memset(lamc[:, :], 1.0))
            c.link(dve.tensor_copy(lamc[HR:ROWS, :], K["neglam"][HR:ROWS, :]))
            SEQ0 = c.n
            for j in range(4):
                dst = qT if j < 2 else kn
                dve.wait_ge(r_turned, j + 1)
                dve.tensor_copy(dst[:, (j % 2) * HH:(j % 2 + 1) * HH, :], t_ps[j % 2][0][:, :, 0:R]).then_inc(r_taken, 1)

            def diagonal(b, first):
                if first:
                    dve.wait_ge(r_taken, 4)
                else:
                    dve.wait_ge(scored, b * (NG + 1))
                for comp in range(2):
                    part = slice(comp * HD, (comp + 1) * HD)
                    diag = qd[part, :].rearrange("p (h x) -> p h x", h=H)[:, :, comp * HR:comp * HR + TS]
                    x = dve.tensor_copy(diag, qT[part, :, ds(b * TS, TS)])
                    x.then_inc(q_ready, 1)

            def pages(b, gs):
                for g in gs:
                    dve.wait_ge(turned, b * 2 * NPG + 2 * g + 2)
                    dve.tensor_copy(kT[g // GP][:, HH:H, (g % GP) * P:(g % GP + 1) * P], t_ps[1][g % 2][:, :, :]
                                    ).then_inc(taken[1], 1)

            def take_a(b):
                dve.wait_ge(a_turned, b + 1)
                dve.tensor_copy(aT[:, 0:NPG * HR], a_ps[:, 0:NPG * HR])
                dve.tensor_copy(aT[0:TS, NPG * HR:], a_ps[0:TS, NPG * HR:]).then_inc(a_taken, 1)

            def reduce(b, place):
                ps = n_ps if place == NG else s_ps[place][:, :]
                cols = slice(PAST, KEYS) if place == NG else slice(place * GP * P, (place + 1) * GP * P)
                if place:
                    dve.wait_ge(reduced, FREE + b * (NG + 1) + place)
                dve.wait_ge(scored, b * (NG + 1) + place + 1)
                dve.sem_inc(passed, 1)
                dve.tensor_tensor_reduce(pr[:, cols], ps, bias[:, cols], -SCALE, low[:, place - 1:place] if place else -BIG,
                                         ALU.add, ALU.min, low[:, place:place + 1]).then_inc(reduced, 1)

            def weigh(b):
                dve.wait_ge(expd, b + 1)
                k = SEQ0 + 2 * b
                dve.reciprocal(rsum[:, :], ssum[:, :]).then_inc(seq, 1)
                dve.wait_ge(seq, k + 1)
                dve.tensor_tensor(coef[:, :], rsum[:, :], lamc[:, :], ALU.mult).then_inc(seq, 1)
                dve.wait_ge(seq, k + 2)
                dve.tensor_scalar(mc[:, :], sel[:, :], coef[:, 0:1], None, ALU.mult).then_inc(mixed, 1)

            diagonal(0, True)
            pages(0, range(NPG))
            for place in range(NG + 1):
                reduce(0, place)
            with dve.Fori(1, NB) as b:
                diagonal(b, False)
                pages(b, range(GP))
                weigh(b - 1)
                pages(b, range(GP, NPG - 1))
                take_a(b - 1)
                pages(b, range(NPG - 1, NPG))
                for place in range(NG + 1):
                    reduce(b, place)
            weigh(NB - 1)
            take_a(NB - 1)

        @block.scalar
        def _(act):
            act.sem_inc(taken[0], FREE)

            def pages(b, first):
                for g in range(NPG):
                    act.wait_ge(turned, b * 2 * NPG + 2 * g + 1)
                    if g % GP == 0 and not first:
                        act.wait_ge(scored, (b - 1) * (NG + 1) + g // GP + 1)
                    act.activation(kT[g // GP][:, 0:HH, (g % GP) * P:(g % GP + 1) * P], t_ps[0][g % 2][:, :, :], ACT.Copy
                                   ).then_inc(taken[0], 1)

            def exp(b):
                act.wait_ge(reduced, FREE + b * (NG + 1) + NG + 1)
                act.activation(pr[:, :], pr[:, :], ACT.Exp, scale=-1.0, bias=low[:, NG:NG + 1], accum_out=ssum[:, :]
                               ).then_inc(expd, 1)

            def result(b, half):
                act.wait_ge(applied, 2 * b + half + 1)
                if half == 0:
                    act.wait_ge(o_out, 16 + b * 16 * H)
                act.activation(o[:, half * HH * P:(half + 1) * HH * P], o_ps[:, :], ACT.Copy).then_inc(o_taken, 1)

            pages(0, True)
            exp(0)
            with act.Fori(1, NB) as b:
                pages(b, False)
                result(b - 1, 0)
                exp(b)
                result(b - 1, 1)
            result(NB - 1, 0)
            result(NB - 1, 1)

        @block.tensor
        def _(pe):
            ident = K["ident"]
            pe.sem_inc(o_taken, FREE)
            pe.wait_ge(row_in, 32)
            for j in range(4):
                src = qrow if j < 2 else krow
                if j >= 2:
                    pe.wait_ge(r_taken, j - 1)
                for h in range(HH):
                    hh = (j % 2) * HH + h
                    x = pe.transpose(t_ps[j % 2][0][:, h, 0:R], src[:, hh * P:(hh + 1) * P], ident[0:R, 0:R])
                x.then_inc(r_turned, 1)
            pe.wait_ge(r_taken, 4)

            def q_of(h):
                return qd[:, h * ROWS:(h + 1) * ROWS]

            def turn(b, g, first):
                pe.wait_ge(k_in[g], 16 * b + 16)
                for j in range(2):
                    if not (first and g < 2):
                        pe.wait_ge(taken[j], FREE + b * NPG + g - 1)
                    for h in range(HH):
                        hh = j * HH + h
                        x = pe.transpose(t_ps[j][g % 2][:, h, :], kp[:, g, hh * P:(hh + 1) * P], ident[:, :])
                    x.then_inc(turned, 1)

            def score(b, n, first):
                for j in range(2):
                    pe.wait_ge(taken[j], FREE + b * NPG + (n + 1) * GP)
                if n == 0:
                    pe.wait_ge(q_ready, 2 * b + 2)
                if not first:
                    pe.wait_ge(reduced, FREE + (b - 1) * (NG + 1) + n + 1)
                for h in range(H):
                    x = pe.matmul(s_ps[n][:, :], q_of(h), kT[n][:, h, :], start=h == 0, stop=h == H - 1)
                x.then_inc(scored, 1)

            def score_new(b, first):
                if not first:
                    pe.wait_ge(a_taken, b)
                for h in range(H):
                    x = pe.matmul(n_ps, q_of(h), kn[:, h, ds(b * TS, TS)], start=h == 0, stop=h == H - 1)
                x.then_inc(scored, 1)

            def turn_a(b):
                pe.wait_ge(mixed, b + 1)
                for g in range(NPG + 1):
                    n = P if g < NPG else TS
                    x = pe.matmul(a_ps[0:n, g * HR:(g + 1) * HR], pr[:, g * P:g * P + n], mc[:, :], start=True, stop=True)
                x.then_inc(a_turned, 1)

            def apply(b, half):
                if half == 0:
                    pe.wait_ge(vn_in, 16 * b + 16)
                    pe.wait_ge(a_taken, b + 1)
                pe.wait_ge(o_taken, FREE + 2 * b + half)
                cols = slice(half * HH * P, (half + 1) * HH * P)
                for g in range(NPG + 1):
                    if half == 0 and g < NPG:
                        pe.wait_ge(v_in[g], 16 * b + 16)
                    n = P if g < NPG else TS
                    v = vp[:, g, cols] if g < NPG else vnew[:, cols]
                    x = pe.matmul(o_ps[:, :], aT[0:n, g * HR:(g + 1) * HR], v, start=g == 0, stop=g == NPG)
                x.then_inc(applied, 1)

            def step(b, first):
                for g in range(NPG):
                    turn(b, g, first)
                    if g % GP == 0 and g:
                        score(b, g // GP - 1, first)
                    if g == NPG - 2 and not first:
                        turn_a(b - 1)
                if not first:
                    apply(b - 1, 0)
                score(b, NG - 1, first)
                score_new(b, first)
                if not first:
                    apply(b - 1, 1)

            step(0, True)
            with pe.Fori(1, NB) as b:
                step(b, False)
            turn_a(NB - 1)
            apply(NB - 1, 0)
            apply(NB - 1, 1)


def last_layer(nc, D, K, full, rest, H):
    w = D["w_out_b"][0]
    KC, N = w.shape[0] // P, w.shape[1]
    pairs = full // 2
    with ExitStack() as ctx:
        m = Memory(nc, ctx, "last")
        wst = [m.sb(f"wst{i}", [P, 2, N]) for i in range(2)]
        wh, wl = m.sb("w_hi", [P, KC, N], F32R), m.sb("w_lo", [P, KC, N], F32R)
        gf = m.sb("gain_f", [P, N])
        o, z, x1, sq, y = ([m.sb(f"{n}{i}", [P, N]) for i in range(2)] for n in ("o", "z", "x1", "sq", "y"))
        gh = [m.sb(f"g_hi{i}", [P, KC, P], F32R) for i in range(2)]
        gl = [m.sb(f"g_lo{i}", [P, KC, P], F32R) for i in range(2)]
        hs, hr, hq = ([m.sb(f"{n}{i}", [P, H]) for i in range(2)] for n in ("head_sum", "head_root", "head_r"))
        ys, yr, yq = ([m.sb(f"{n}{i}", [P, 1]) for i in range(2)] for n in ("row_sum", "row_root", "row_r"))
        t_ps = [m.ps(f"t{i}", [P, KC, P]) for i in range(2)]
        acc = [m.ps(f"acc{i}", [P, N]) for i in range(2)]
        w_sem, oz_sem, x_sem, out_sem = ([m.sem(f"{n}{i}") for i in range(2)] for n in ("w_in", "oz_in", "x1_in", "out"))
        (gf_in, whi, wlo, gated_z, squared, h_mean, h_root, seq, gated, turned, g_hi, g_lo, mm, added, y_sq, y_mean, y_root,
         recip, done) = (m.sem(n) for n in (
             "gf_in", "whi", "wlo", "gated_z", "squared", "h_mean", "h_root", "seq", "gated", "turned", "ghi", "glo", "mm",
             "added", "y_sq", "y_mean", "y_root", "recip", "done"))
        block = m.block()
        wv = w.rearrange("(k p) n -> p k n", p=P)

        def run(eng, pre, mid, post):
            def pair(b, rows_ahead=P):
                mid(b + 1, 1, P)
                pre(b + 2, 0, rows_ahead)
                post(b, 0, P)
                mid(b + 2, 0, rows_ahead)
                if rows_ahead == P:
                    pre(b + 3, 1, P)
                post(b + 1, 1, P)

            pre(0, 0, P)
            mid(0, 0, P)
            pre(1, 1, P)
            pair(0)
            with eng.Fori(1, pairs - 1) as i:
                pair(2 * i)
            pair(full - 2, rest)
            post(full, 0, rest)

        def nothing(b, s, n):
            pass

        @block.sync
        def _(sp):
            def load_oz(b, s, n=P):
                if not (isinstance(b, int) and b < 2):
                    sp.wait_ge(turned, b - 1)
                for src, t in ((D["o_rows"], o), (D["z_rows"], z)):
                    sp.dma_start(t[s][0:n, :], src[ds(b * P, n), :]).then_inc(oz_sem[s], 16)

            def load_x1(b, s, n=P):
                sp.dma_start(x1[s][0:n, :], D["x1"][ds(b * P, n), :]).then_inc(x_sem[s], 16)

            def store(b, s, n=P):
                sp.wait_ge(done, b + 1)
                dst = D["y_rows"][ds(b * P, P), :] if n == P else D["ys_rows"]
                sp.dma_start(dst, y[s][0:n, :]).then_inc(out_sem[s], 16)

            load_oz(0, 0)
            load_oz(1, 1)
            for j in range(KC // 2):
                if j >= 2:
                    sp.wait_ge(wlo, 2 * (j - 1))
                sp.dma_start(wst[j % 2][:, :, :], wv[:, 2 * j:2 * j + 2, :]).then_inc(w_sem[j % 2], 16)
            load_x1(0, 0)
            load_x1(1, 1)
            sp.dma_start(gf[:, :], D["norm_f_g"].partition_broadcast(P)).then_inc(gf_in, 16)
            load_oz(2, 0)
            load_oz(3, 1)
            store(0, 0)
            load_x1(2, 0)
            with sp.Fori(2, pairs) as i:
                load_oz(2 * i, 0)
                store(2 * i - 3, 1)
                load_x1(2 * i - 1, 1)
                load_oz(2 * i + 1, 1)
                store(2 * i - 2, 0)
                load_x1(2 * i, 0)
            load_oz(full, 0, rest)
            store(full - 3, 1)
            load_x1(full - 1, 1)
            store(full - 2, 0)
            load_x1(full, 0, rest)
            store(full - 1, 1)
            store(full, 0, rest)
            sp.wait_ge(out_sem[0], 16 * (pairs + 1))
            sp.wait_ge(out_sem[1], 16 * pairs)

        @block.gpsimd
        def _(pool):
            def gate(b, s, n):
                pool.wait_ge(oz_sem[s], 16 * (b - s) + 32)
                pool.tensor_tensor(z[s][0:n, :], o[s][0:n, :], z[s][0:n, :], ALU.mult).then_inc(gated_z, 1)

            run(pool, gate, nothing, nothing)

        @block.scalar
        def _(act):
            for k in range(KC):
                act.wait_ge(w_sem[(k // 2) % 2], 16 * (k // 4) + 16)
                act.activation(wh[:, k, :], wst[(k // 2) % 2][:, k % 2, :], ACT.Copy, scale=K["gain_v"][:, 0:1]).then_inc(whi, 1)

            def pre(b, s, n):
                act.wait_ge(oz_sem[s], 16 * (b - s) + 32)
                if not (isinstance(b, int) and b < 4):
                    act.wait_ge(y_sq, b - 3)
                act.activation(sq[s][0:n, :], o[s][0:n, :], ACT.Square).then_inc(squared, 1)
                act.wait_ge(h_mean, b + 1)
                act.activation(hr[s][0:n, :], hs[s][0:n, :], ACT.Sqrt).then_inc(h_root, 1)

            def mid(b, s, n):
                act.wait_ge(turned, b + 1)
                if not (isinstance(b, int) and b < 2):
                    act.wait_ge(mm, b - 1)
                act.activation(gh[s][:, :, 0:n], t_ps[s][:, :, 0:n], ACT.Copy).then_inc(g_hi, 1)

            def post(b, s, n):
                act.wait_ge(added, b + 1)
                act.activation(sq[s][0:n, :], x1[s][0:n, :], ACT.Square, accum_out=ys[s][0:n, :]).then_inc(y_sq, 1)
                act.wait_ge(y_mean, b + 1)
                act.activation(yr[s][0:n, :], ys[s][0:n, :], ACT.Sqrt).then_inc(y_root, 1)

            run(act, pre, mid, post)

        @block.vector
        def _(dve):
            for k in range(KC):
                dve.wait_ge(whi, k + 1)
                dve.scalar_tensor_tensor(out=wl[:, k, :], in0=wst[(k // 2) % 2][:, k % 2, :], scalar=K["gain_v"][:, 0:1],
                                         in1=f32(wh[:, k, :]), op0=ALU.mult, op1=ALU.subtract).then_inc(wlo, 1)

            def pre(b, s, n):
                k = 2 * b
                heads = lambda t: t[0:n, :].rearrange("p (h v) -> p h v", h=H)
                dve.wait_ge(squared, b + 1)
                dve.tensor_reduce(hs[s][0:n, :], heads(sq[s]), AX_X, ALU.add).then_inc(seq, 1)
                dve.wait_ge(seq, k + 1)
                dve.tensor_scalar(hs[s][0:n, :], hs[s][0:n, :], float(H) / N, EPS, ALU.mult, ALU.add).then_inc(h_mean, 1)
                dve.wait_ge(h_root, b + 1)
                dve.reciprocal(hq[s][0:n, :], hr[s][0:n, :]).then_inc(seq, 1)
                dve.wait_ge(seq, k + 2)
                dve.wait_ge(gated_z, b + 1)
                dve.tensor_tensor(heads(o[s]), heads(z[s]), hq[s][0:n, :].unsqueeze(2).broadcast_to([n, H, N // H]),
                                  ALU.mult).then_inc(gated, 1)

            def mid(b, s, n):
                dve.wait_ge(g_hi, b + 1)
                dve.tensor_tensor(gl[s][:, :, 0:n], t_ps[s][:, :, 0:n], f32(gh[s][:, :, 0:n]), ALU.subtract).then_inc(g_lo, 1)

            def post(b, s, n):
                dve.wait_ge(mm, b + 1)
                dve.wait_ge(x_sem[s], 8 * (b - s) + 16)
                dve.tensor_tensor(x1[s][0:n, :], acc[s][0:n, :], x1[s][0:n, :], ALU.add).then_inc(added, 1)
                dve.wait_ge(y_sq, b + 1)
                dve.tensor_scalar(ys[s][0:n, :], ys[s][0:n, :], 1.0 / N, EPS, ALU.mult, ALU.add).then_inc(y_mean, 1)
                dve.wait_ge(y_root, b + 1)
                dve.reciprocal(yq[s][0:n, :], yr[s][0:n, :]).then_inc(recip, 1)
                dve.wait_ge(recip, b + 1)
                if isinstance(b, int) and b == 0:
                    dve.wait_ge(gf_in, 16)
                if not (isinstance(b, int) and b < 2):
                    dve.wait_ge(out_sem[s], 8 * (b - s))
                dve.scalar_tensor_tensor(out=y[s][0:n, :], in0=x1[s][0:n, :], scalar=yq[s][0:n, 0:1], in1=gf[0:n, :],
                                         op0=ALU.mult, op1=ALU.mult).then_inc(done, 1)

            run(dve, pre, mid, post)

        @block.tensor
        def _(pe):
            ident = K["ident"]

            def mid(b, s, n):
                pe.wait_ge(gated, b + 1)
                if not (isinstance(b, int) and b < 2):
                    pe.wait_ge(g_lo, b - 1)
                for k in range(KC):
                    x = pe.transpose(t_ps[s][:, k, 0:n], o[s][0:n, k * P:(k + 1) * P], ident[0:n, 0:n])
                x.then_inc(turned, 1)

            def post(b, s, n):
                pe.wait_ge(g_lo, b + 1)
                if not (isinstance(b, int) and b < 2):
                    pe.wait_ge(added, b - 1)
                for k in range(KC):
                    if isinstance(b, int) and b == 0:
                        pe.wait_ge(wlo, k + 1)
                    for c in range(N // 512):
                        cols = slice(c * 512, (c + 1) * 512)
                        last = three(pe, acc[s][0:n, cols], gh[s][:, k, 0:n], gl[s][:, k, 0:n],
                                     wh[:, k, cols], wl[:, k, cols], k == 0, k == KC - 1)
                last.then_inc(mm, 1)

            run(pe, nothing, mid, post)


def program(nc, D):
    S, DM = D["x_prompt"].shape[1:]
    NB, TS = D["x_sample"].shape[:2]
    R = NB * TS
    NT = S + R
    DA = D["w_in_a"].shape[2] // 2
    half = S // 2
    KC = DM // P
    D["gatedT"] = nc.dram_tensor("gatedT", (DA, NT), F32, kind="Internal").ap()
    for n in ("x1", "q_rows", "z_rows", "o_rows"):
        D[n] = nc.dram_tensor(n, (NT, DM), F32, kind="Internal").ap()
    for n in ("k_twice", "q_twice"):
        D[n] = nc.dram_tensor(n, (S, 2 * DM), F32, kind="Internal").ap()
    x_sample = D["x_sample"].rearrange("b t n -> (b t) n")
    for n in "kv":
        D[n + "_prompt"] = D[f"{n}_prompt_pages"].rearrange("b g p h d -> (b g p) (h d)")
        D[n + "_sample"] = D[f"{n}_sample_rows"].rearrange("b t h d -> (b t) (h d)")

    D["y_rows"] = D["y_prompt"].rearrange("b s n -> (b s) n")
    D["ys_rows"] = D["y_sample"].rearrange("b t n -> (b t) n")

    with ExitStack() as ctx:
        m = Memory(nc, ctx, "all")
        K = {"ident": m.sb("ident", [P, P]), "neglam": m.sb("neg_lambda", [P, 1]), "gain_v": m.sb("gain_v", [P, 1]),
             "gain_kv": m.sb("gain_kv", [P, KC]), "gain_b": m.sb("gain_b", [P, KC])}
        with ExitStack() as front:
            f = Memory(nc, front, "front")
            K["win"] = f.sb("windows", [P, len(WINDOWS) * WROW])
            K["scale"] = f.sb("scale_a", [P, DA // P])
            K["carry"], K["carry2"] = f.sb("zeros", [P, DA // P, HIST]), f.sb("carry", [P, DA // P, HIST])
            K["stateT"] = f.sb("stateT", [P, DA // P, NB * HIST])
            K["tails"] = f.sb("tails", [P, DA // P, HIST + R])
            setup(nc, D, K)
            for h, T in enumerate((half, half + R)):
                with ExitStack() as part:
                    x = Memory(nc, part, f"a{h}")
                    xh, xl = x.sb("x_hi", [P, KC, T], F32R), x.sb("x_lo", [P, KC, T], F32R)
                    t0 = h * half
                    blocks = [(D["x_prompt"][0, t0 + b * P:t0 + (b + 1) * P, :], P) for b in range(half // P)]
                    if h:
                        blocks.append((x_sample, R))
                    pool_layer(nc, h, D, K, xh, xl, blocks, T, half, t0, K["carry"] if h == 0 else K["carry2"],
                               K["carry2"])
            tails(nc, D, K, R)
        out_layer(nc, D, S // P, R, x_sample)
        gains = [K["gain_kv"], K["gain_b"]]
        for h, T in enumerate((half, half + R)):
            with ExitStack() as sub:
                x = Memory(nc, sub, f"b{h}")
                xh, xl = x.sb("x_hi", [P, KC, T], F32R), x.sb("x_lo", [P, KC, T], F32R)
                t0 = h * half
                blocks = [(D["x1"][t0 + b * P:t0 + min((b + 1) * P, T), :], min(P, T - b * P)) for b in range(-(-T // P))]
                project(nc, h, D, K, xh, xl, blocks, T, half, t0, gains)
        H = D["cache_k"].shape[2]
        attention(nc, D, K, S, H)
        sample_attention(nc, D, K, S, H, NB, TS)
        last_layer(nc, D, K, S // P, R, H)


_INS = ["x_prompt", "x_sample", "cache_k", "cache_v", "state_pool", "page_table", "norm_a_g", "w_in_a", "w_map_a",
        "scale_a", "w_out_a", "norm_kv_g", "w_kv", "norm_b_g", "w_in_b", "lambda_q1", "lambda_k1", "lambda_q2",
        "lambda_k2", "subln_g", "w_out_b", "norm_f_g"]


def kernel(**inputs):
    import concourse.bacc as bacc
    from concourse.bass_utils import run_bass_kernel_spmd as run

    nc = bacc.Bacc("TRN2", target_bir_lowering=False, num_devices=1)
    arrays, D = {}, {}
    for name in _INS:
        a = np.ascontiguousarray(inputs[name])
        arrays[f"in_{name}"] = a
        D[name] = nc.dram_tensor(f"in_{name}", a.shape, mybir.dt.from_np(a.dtype), kind="ExternalInput").ap()
    (B, S, DM), (DB, TS, _) = inputs["x_prompt"].shape, inputs["x_sample"].shape
    _, page, H, KD = inputs["cache_k"].shape
    VD = inputs["cache_v"].shape[3]
    L, _, hist, DA = inputs["state_pool"].shape
    outs = {
        "y_prompt": (B, S, DM), "y_sample": (DB, TS, DM),
        "k_prompt_pages": (B, S // page, page, H, KD), "v_prompt_pages": (B, S // page, page, H, VD),
        "k_sample_rows": (DB, TS, H, KD), "v_sample_rows": (DB, TS, H, VD),
        "pool_prompt": (L, B, hist, DA), "pool_sample": (L, DB, hist, DA),
    }
    for name, shape in outs.items():
        D[name] = nc.dram_tensor(f"out_{name}", shape, F32, kind="ExternalOutput").ap()
    program(nc, D)
    r = run(nc, [arrays], core_ids=[0])
    return tuple(r.results[0][f"out_{name}"] for name in outs)
```
